# Optimizing a Trainium2 kernel written in Bass

```python
import functools
import jax, jax.numpy as jnp
from jax import lax
import numpy as np

D_MODEL = 2048
BATCH = 1
SEQ = 256
DEPTH = 1
DEC_BATCH = 8
DEC_SEQ = 1
PAST_LEN = 2048
PAGE_SIZE = 128

HEAD_DIM = 64
ATT_W = D_MODEL // 4
RWKV_W = (3 * D_MODEL) // 8
CONV_W = D_MODEL - ATT_W - RWKV_W
ATT_HEADS = ATT_W // HEAD_DIM
RWKV_HEADS = RWKV_W // HEAD_DIM
W_LORA = 64
A_LORA = 64
G_LORA = 128
RWKV_PROJ = 3 * RWKV_W + W_LORA + A_LORA + G_LORA
MIX_PROJ = 3 * ATT_W + RWKV_PROJ + 3 * CONV_W
D_FF = ((8 * D_MODEL) // 3 + 255) // 256 * 256
CONV_K = 3
DILATION_GROUPS = ((128, 1), (512, 4), (2048, 16))
SWA_BUF = 2048
NORM_EPS = 1e-6
RWKV_GN_EPS = 64e-5

kernel_name = "hybrid_rwkv7_dilated_swa_shortconv_step"

def rms_norm(x, g):
    xf = x.astype(jnp.float32)
    xf = xf * lax.rsqrt(jnp.mean(xf * xf, axis=-1, keepdims=True) + NORM_EPS)
    return (xf * g.astype(jnp.float32)).astype(x.dtype)

def swiglu(h, w_gate, w_up, w_down):
    return (jax.nn.silu(h @ w_gate) * (h @ w_up)) @ w_down

def alibi_slopes():
    return 2.0 ** (-8.0 * jnp.arange(1, ATT_HEADS + 1, dtype=jnp.float32) / ATT_HEADS)

def dilated_group_prompt(q, k, v, window, dil, slopes):
    n, t, nh, e = q.shape
    span = window // dil
    sub = t // dil
    nb = -(-sub // span)
    sub_p = nb * span

    def to_blocks(a):
        a = a.reshape(n, sub, dil, nh, e).transpose(0, 2, 1, 3, 4)
        a = jnp.pad(a, ((0, 0), (0, 0), (0, sub_p - sub), (0, 0), (0, 0)))
        return a.reshape(n, dil, nb, span, nh, e)

    def with_prev_block(a):
        prev = jnp.pad(a, ((0, 0), (0, 0), (1, 0), (0, 0), (0, 0), (0, 0)))[:, :, :-1]
        return jnp.concatenate([prev, a], axis=3)

    qb = to_blocks(q)
    kb = with_prev_block(to_blocks(k))
    vb = with_prev_block(to_blocks(v))
    s = jnp.einsum('nrbqhe,nrbkhe->nrbhqk', qb, kb,
                   preferred_element_type=jnp.float32) * (HEAD_DIM ** -0.5)
    qi = jnp.arange(span)[:, None]
    ki = jnp.arange(2 * span)[None, :]
    steps = qi + span - ki
    key_sub = jnp.arange(nb)[:, None, None] * span + ki[None] - span
    valid = (steps >= 0) & (steps <= span) & (key_sub >= 0)
    s = s - slopes[:, None, None] * (dil * steps).astype(jnp.float32)
    s = jnp.where(valid[None, None, :, None], s, -jnp.inf)
    lse = jax.nn.logsumexp(s, axis=-1)
    p = jnp.exp(s - lse[..., None]).astype(v.dtype)
    o = jnp.einsum('nrbhqk,nrbkhe->nrbqhe', p, vb)
    o = o.reshape(n, dil, sub_p, nh, e)[:, :, :sub].transpose(0, 2, 1, 3, 4).reshape(n, t, nh, e)
    lse = lse.transpose(0, 1, 2, 4, 3).reshape(n, dil, sub_p, nh)[:, :, :sub]
    lse = lse.transpose(0, 2, 1, 3).reshape(n, t, nh)
    return o, lse

def dilated_group_sample(q, k_all, v_all, past, window, dil, slopes):
    tn = q.shape[1]
    span = window // dil
    j = jnp.arange(span + 1)
    idx = past + jnp.arange(tn)[:, None] - dil * j[None, :]
    valid = idx >= 0
    idx = jnp.maximum(idx, 0)
    kg = k_all[:, idx]
    vg = v_all[:, idx]
    s = jnp.einsum('nqhe,nqjhe->nqhj', q, kg,
                   preferred_element_type=jnp.float32) * (HEAD_DIM ** -0.5)
    s = s - slopes[:, None] * (dil * j).astype(jnp.float32)[None, :]
    s = jnp.where(valid[None, :, None, :], s, -jnp.inf)
    lse = jax.nn.logsumexp(s, axis=-1)
    p = jnp.exp(s - lse[..., None]).astype(v_all.dtype)
    o = jnp.einsum('nqhj,nqjhe->nqhe', p, vg)
    return o, lse

def merge_groups(outs, lses):
    wts = jax.nn.softmax(jnp.stack(lses, axis=-1), axis=-1)
    o = outs[0].astype(jnp.float32) * wts[..., 0:1]
    for g in range(1, len(outs)):
        o = o + outs[g].astype(jnp.float32) * wts[..., g:g + 1]
    return o.astype(outs[0].dtype)

def attend_prompt(q, k, v):
    slopes = alibi_slopes()
    outs, lses = [], []
    for window, dil in DILATION_GROUPS:
        o, l = dilated_group_prompt(q, k, v, window, dil, slopes)
        outs.append(o)
        lses.append(l)
    keep = min(SWA_BUF, q.shape[1])
    return merge_groups(outs, lses), k[:, -keep:], v[:, -keep:]

def attend_sample(q, k, v, buf_k, buf_v):
    slopes = alibi_slopes()
    past = buf_k.shape[1]
    k_all = jnp.concatenate([buf_k.astype(k.dtype), k], axis=1)
    v_all = jnp.concatenate([buf_v.astype(v.dtype), v], axis=1)
    outs, lses = [], []
    for window, dil in DILATION_GROUPS:
        o, l = dilated_group_sample(q, k_all, v_all, past, window, dil, slopes)
        outs.append(o)
        lses.append(l)
    return merge_groups(outs, lses), k, v

def wkv7_scan(s0, r, w, k, v, a, b):
    def step(s, inp):
        r_t, w_t, k_t, v_t, a_t, b_t = inp
        sa = jnp.einsum('nhvk,nhk->nhv', s, a_t)
        s = s * w_t[:, :, None, :] + sa[..., None] * b_t[:, :, None, :] + v_t[..., None] * k_t[:, :, None, :]
        return s, jnp.einsum('nhvk,nhk->nhv', s, r_t)
    xs = tuple(jnp.moveaxis(z, 1, 0) for z in (r, w, k, v, a, b))
    s, ys = lax.scan(step, s0, xs)
    return jnp.moveaxis(ys, 0, 1), s

def token_mixers(h, lp, shift_prev, wkv0, conv_prev, attend):
    n, t, _ = h.shape
    f32 = jnp.float32
    p = h @ lp['w_in']
    o1 = 3 * ATT_W
    o2 = o1 + RWKV_PROJ
    p_att, p_rwkv, p_conv = p[..., :o1], p[..., o1:o2], p[..., o2:]

    ah = (n, t, ATT_HEADS, HEAD_DIM)
    q = rms_norm(p_att[..., :ATT_W].reshape(ah), lp['q_norm'])
    k = rms_norm(p_att[..., ATT_W:2 * ATT_W].reshape(ah), lp['k_norm'])
    v = p_att[..., 2 * ATT_W:].reshape(ah)
    o_att, k_rows, v_rows = attend(q, k, v)

    prev = jnp.concatenate([shift_prev[:, None, :].astype(p_rwkv.dtype), p_rwkv[:, :-1]], axis=1)
    xm = p_rwkv + (prev - p_rwkv) * lp['rwkv_mu']
    c1, c2, c3 = RWKV_W, 2 * RWKV_W, 3 * RWKV_W
    r = xm[..., :c1]
    kr = xm[..., c1:c2]
    vr = xm[..., c2:c3]
    wl = xm[..., c3:c3 + W_LORA]
    al = xm[..., c3 + W_LORA:c3 + W_LORA + A_LORA]
    gl = xm[..., c3 + W_LORA + A_LORA:]
    w_log = -jax.nn.softplus(-(lp['rwkv_w0'] + jnp.tanh(wl) @ lp['rwkv_w2']).astype(f32)) - 0.5
    decay = jnp.exp(-jnp.exp(w_log))
    a = jax.nn.sigmoid((lp['rwkv_a0'] + al @ lp['rwkv_a2']).astype(f32))
    g = (jax.nn.sigmoid(gl) @ lp['rwkv_g2']).astype(f32)
    rh = (n, t, RWKV_HEADS, HEAD_DIM)
    krf = kr.astype(f32)
    kk = (krf * lp['rwkv_k_k']).reshape(rh)
    kk = kk / jnp.maximum(jnp.sqrt(jnp.sum(kk * kk, axis=-1, keepdims=True)), 1e-12)
    kmod = (krf * (1.0 + (a - 1.0) * lp['rwkv_k_a'])).reshape(rh)
    rf = r.astype(f32).reshape(rh)
    vf = vr.astype(f32).reshape(rh)
    y, wkv_new = wkv7_scan(wkv0.astype(f32), rf, decay.reshape(rh), kmod, vf, -kk, kk * a.reshape(rh))
    mu_y = jnp.mean(y, axis=-1, keepdims=True)
    var_y = jnp.mean(jnp.square(y - mu_y), axis=-1, keepdims=True)
    y = ((y - mu_y) * lax.rsqrt(var_y + RWKV_GN_EPS)).reshape(n, t, RWKV_W)
    y = y * lp['rwkv_ln_w'] + lp['rwkv_ln_b']
    bonus = jnp.sum(rf * kmod * lp['rwkv_r_k'], axis=-1, keepdims=True) * vf
    y_rwkv = ((y + bonus.reshape(n, t, RWKV_W)) * g).astype(h.dtype)
    shift_new = p_rwkv[:, -1]

    u = p_conv[..., :CONV_W]
    gate_b = p_conv[..., CONV_W:2 * CONV_W]
    gate_c = p_conv[..., 2 * CONV_W:]
    z = gate_c * u
    zc = jnp.concatenate([conv_prev.astype(z.dtype), z], axis=1)
    yc = lp['conv_b']
    for i in range(CONV_K):
        yc = yc + lp['conv_w'][i] * zc[:, i:i + t]
    y_conv = gate_b * yc
    conv_new = zc[:, -(CONV_K - 1):]

    mix = jnp.concatenate([o_att.reshape(n, t, ATT_W), y_rwkv, y_conv.astype(h.dtype)], axis=-1) @ lp['w_out']
    return mix, (k_rows, v_rows, wkv_new, shift_new, conv_new)

def trunk_layer(x, lp, shift_prev, wkv0, conv_prev, attend):
    x = x + 0.5 * swiglu(rms_norm(x, lp['ffn1_norm']), lp['ffn1_w_gate'], lp['ffn1_w_up'], lp['ffn1_w_down'])
    mix, new_state = token_mixers(rms_norm(x, lp['mix_norm']), lp, shift_prev, wkv0, conv_prev, attend)
    x = x + mix
    x = x + 0.5 * swiglu(rms_norm(x, lp['ffn2_norm']), lp['ffn2_w_gate'], lp['ffn2_w_up'], lp['ffn2_w_down'])
    return x, new_state

def setup_inputs(seed: int = 0) -> dict:
    key = jax.random.key(seed)
    keys = iter(jax.random.split(key, 40))
    f32 = jnp.float32

    def nrm(shape, scale=1.0):
        return scale * jax.random.normal(next(keys), shape, f32)

    def gain(shape):
        return 1.0 + 0.02 * jax.random.normal(next(keys), shape, f32)

    def unif(shape, lo, hi):
        return jax.random.uniform(next(keys), shape, f32, lo, hi)

    swa_len = min(SWA_BUF, PAST_LEN)
    return {
        'x_prompt': nrm((BATCH, SEQ, D_MODEL)),
        'x_sample': nrm((DEC_BATCH, DEC_SEQ, D_MODEL)),
        'cache_swa_k': nrm((DEPTH, DEC_BATCH, swa_len, ATT_HEADS, HEAD_DIM)),
        'cache_swa_v': nrm((DEPTH, DEC_BATCH, swa_len, ATT_HEADS, HEAD_DIM)),
        'state_wkv': nrm((DEPTH, DEC_BATCH, RWKV_HEADS, HEAD_DIM, HEAD_DIM), 0.3),
        'state_shift': nrm((DEPTH, DEC_BATCH, RWKV_PROJ)),
        'state_conv': nrm((DEPTH, DEC_BATCH, CONV_K - 1, CONV_W)),
        'ffn1_norm': gain((DEPTH, D_MODEL)),
        'ffn1_w_gate': nrm((DEPTH, D_MODEL, D_FF), D_MODEL ** -0.5),
        'ffn1_w_up': nrm((DEPTH, D_MODEL, D_FF), D_MODEL ** -0.5),
        'ffn1_w_down': nrm((DEPTH, D_FF, D_MODEL), D_FF ** -0.5),
        'mix_norm': gain((DEPTH, D_MODEL)),
        'w_in': nrm((DEPTH, D_MODEL, MIX_PROJ), D_MODEL ** -0.5),
        'q_norm': gain((DEPTH, HEAD_DIM)),
        'k_norm': gain((DEPTH, HEAD_DIM)),
        'rwkv_mu': unif((DEPTH, RWKV_PROJ), 0.0, 1.0),
        'rwkv_w0': unif((DEPTH, RWKV_W), -6.0, 1.0),
        'rwkv_w2': nrm((DEPTH, W_LORA, RWKV_W), 0.5 * W_LORA ** -0.5),
        'rwkv_a0': nrm((DEPTH, RWKV_W), 0.5),
        'rwkv_a2': nrm((DEPTH, A_LORA, RWKV_W), A_LORA ** -0.5),
        'rwkv_g2': nrm((DEPTH, G_LORA, RWKV_W), G_LORA ** -0.5),
        'rwkv_k_k': 0.85 + nrm((DEPTH, RWKV_W), 0.05),
        'rwkv_k_a': 1.0 + nrm((DEPTH, RWKV_W), 0.05),
        'rwkv_r_k': nrm((DEPTH, RWKV_HEADS, HEAD_DIM), 0.1),
        'rwkv_ln_w': gain((DEPTH, RWKV_W)),
        'rwkv_ln_b': nrm((DEPTH, RWKV_W), 0.02),
        'conv_w': nrm((DEPTH, CONV_K, CONV_W), CONV_K ** -0.5),
        'conv_b': nrm((DEPTH, CONV_W), 0.02),
        'w_out': nrm((DEPTH, D_MODEL, D_MODEL), D_MODEL ** -0.5),
        'ffn2_norm': gain((DEPTH, D_MODEL)),
        'ffn2_w_gate': nrm((DEPTH, D_MODEL, D_FF), D_MODEL ** -0.5),
        'ffn2_w_up': nrm((DEPTH, D_MODEL, D_FF), D_MODEL ** -0.5),
        'ffn2_w_down': nrm((DEPTH, D_FF, D_MODEL), D_FF ** -0.5),
    }

def reference(x_prompt, x_sample, cache_swa_k, cache_swa_v, state_wkv, state_shift, state_conv,
              ffn1_norm, ffn1_w_gate, ffn1_w_up, ffn1_w_down, mix_norm, w_in, q_norm, k_norm,
              rwkv_mu, rwkv_w0, rwkv_w2, rwkv_a0, rwkv_a2, rwkv_g2, rwkv_k_k, rwkv_k_a, rwkv_r_k,
              rwkv_ln_w, rwkv_ln_b, conv_w, conv_b, w_out,
              ffn2_norm, ffn2_w_gate, ffn2_w_up, ffn2_w_down):
    xp, xs = x_prompt, x_sample
    n_p = xp.shape[0]
    p_states, s_states = [], []
    for l in range(DEPTH):
        lp = {
            'ffn1_norm': ffn1_norm[l], 'ffn1_w_gate': ffn1_w_gate[l], 'ffn1_w_up': ffn1_w_up[l],
            'ffn1_w_down': ffn1_w_down[l], 'mix_norm': mix_norm[l], 'w_in': w_in[l],
            'q_norm': q_norm[l], 'k_norm': k_norm[l], 'rwkv_mu': rwkv_mu[l], 'rwkv_w0': rwkv_w0[l],
            'rwkv_w2': rwkv_w2[l], 'rwkv_a0': rwkv_a0[l], 'rwkv_a2': rwkv_a2[l], 'rwkv_g2': rwkv_g2[l],
            'rwkv_k_k': rwkv_k_k[l], 'rwkv_k_a': rwkv_k_a[l], 'rwkv_r_k': rwkv_r_k[l],
            'rwkv_ln_w': rwkv_ln_w[l], 'rwkv_ln_b': rwkv_ln_b[l], 'conv_w': conv_w[l],
            'conv_b': conv_b[l], 'w_out': w_out[l], 'ffn2_norm': ffn2_norm[l],
            'ffn2_w_gate': ffn2_w_gate[l], 'ffn2_w_up': ffn2_w_up[l], 'ffn2_w_down': ffn2_w_down[l],
        }
        xp, st_p = trunk_layer(xp, lp,
                               jnp.zeros((n_p, RWKV_PROJ), xp.dtype),
                               jnp.zeros((n_p, RWKV_HEADS, HEAD_DIM, HEAD_DIM), jnp.float32),
                               jnp.zeros((n_p, CONV_K - 1, CONV_W), xp.dtype),
                               attend_prompt)
        p_states.append(st_p)
        xs, st_s = trunk_layer(xs, lp, state_shift[l], state_wkv[l], state_conv[l],
                               functools.partial(attend_sample, buf_k=cache_swa_k[l], buf_v=cache_swa_v[l]))
        s_states.append(st_s)

    def stacked(states, i):
        return jnp.stack([st[i] for st in states], axis=0)

    prompt_swa_k = stacked(p_states, 0)
    prompt_swa_v = stacked(p_states, 1)
    prompt_wkv = stacked(p_states, 2)
    prompt_shift = stacked(p_states, 3)
    prompt_conv = stacked(p_states, 4)
    sample_swa_k = stacked(s_states, 0)
    sample_swa_v = stacked(s_states, 1)
    sample_wkv = stacked(s_states, 2)
    sample_shift = stacked(s_states, 3)
    sample_conv = stacked(s_states, 4)
    return (xp, xs, prompt_swa_k, prompt_swa_v, prompt_wkv, prompt_shift, prompt_conv,
            sample_swa_k, sample_swa_v, sample_wkv, sample_shift, sample_conv)


_drawn_inputs = setup_inputs


def setup_inputs(seed=0):
    import zlib

    import numpy as np

    out = dict(_drawn_inputs(seed))
    spreads = {}
    factors = {'ffn1_norm': 4.497,
     'q_norm': 64.0,
     'k_norm': 8.58,
     'rwkv_ln_w': 44.107,
     'rwkv_ln_b': 44.901,
     'conv_b': 27.126,
     'ffn2_norm': 8.0,
     'rwkv_r_k': 3.935}
    for name, (base, spread) in spreads.items():
        noise = np.random.default_rng([zlib.crc32(name.encode()), seed]).standard_normal(out[name].shape)
        drawn = base * np.exp(spread * noise) if base else spread * noise
        out[name] = __import__('jax').numpy.asarray(drawn.astype(out[name].dtype))
    for name, factor in factors.items():
        out[name] = (out[name] * factor).astype(out[name].dtype)
    return out
```

```python
from contextlib import ExitStack

import numpy as np

import concourse.bass as bass
from concourse import mybir

F32 = mybir.dt.float32
F32R = mybir.dt.float32r
U32 = mybir.dt.uint32
ACT = mybir.ActivationFunctionType
ALU = mybir.AluOpType
AX = mybir.AxisListType

P = 128
D = 2048
FF = 5632
MIX = 6400
T = 256
NB = 8
N = T + NB
KT = D // P
FT = FF // P
MT = MIX // P
CK = 4
CW = 2 * P
RING = 4
RW = 768
RT = RW // P
H = 12
C = 64
PAST = 2048
EPS = 1e-6
GN_EPS = 64e-5
DECAY = float(np.exp(-0.5))
DILATIONS = (1, 4, 16)
SPAN = 128

GU_PER, DN_PER, IN_PER, OUT_PER = 8, 12, 4, 4
GU1 = 0
DN1 = GU1 + GU_PER * FT // 2
IN = DN1 + DN_PER * KT // 2
OUT = IN + IN_PER * MT // 2
GU2 = OUT + OUT_PER * KT // 2
DN2 = GU2 + GU_PER * FT // 2
DN_KT = [4] * 8 + [3] * 4
DN_K0 = [sum(DN_KT[:k]) for k in range(DN_PER)]

VA = dict(ffn1=0, mix=16, ffn2=32, mu=48)
VB = dict(w0=0, a0=6, kk=12, ka=18, rk=24, lnw=30, lnb=36, cw=42, cb=60, qn=66, kn=67)


def slope(h):
    return float(2.0 ** (-8.0 * (h + 1) / 8))


def tables():
    q = np.arange(P)[:, None]
    k = np.arange(P)[None, :]
    own = q - k
    dist = np.concatenate([own, own + P, own], 1)
    mult = ((dist >= 0) & (dist <= SPAN)).astype(np.float32)
    for dil in DILATIONS[1:]:
        mult += (dist >= 0) & (dist % dil == 0)
    dist = np.where(mult > 0, dist, 1e30).astype(np.float32)
    ident = np.eye(P, dtype=np.float32)
    blk = np.kron(np.eye(2), np.ones((C, C))).astype(np.float32)
    i64 = np.concatenate([np.eye(C), np.eye(C)], 0).astype(np.float32)
    r = (np.arange(P) % C)[:, None]
    c = np.arange(C)[None, :]
    m = [i64, (r < c), (r <= c), (r > c)]
    for s in (1, 2, 4, 8, 16, 32):
        up = (r // s % 2 == 0) & (c // s == r // s + 1)
        lo = (c // s % 2 == 0) & (r // s == c // s + 1)
        m += [up, lo]
    masks = np.concatenate([x.astype(np.float32) for x in m], 1)
    alibi = np.zeros((32, 2, 3, P), np.float32)
    for bj in range(32):
        for par in range(2):
            for g, dil in enumerate(DILATIONS):
                alibi[bj, par, g] = -slope(2 * (bj % 4) + par) * dil * (P - np.arange(P))
    rows = np.arange(96)
    gather = (rows[:, None] // 2 == np.arange(48)[None, :]).astype(np.float32)
    parity = (rows[:, None] % 2 == np.arange(2)[None, :]).astype(np.float32)
    return {
        "c_base": np.concatenate([ident, blk], 1),
        "c_att": np.concatenate([dist, mult], 1),
        "c_masks": masks,
        "c_alibi": alibi.reshape(32, 768),
        "c_gather": np.concatenate([gather, parity], 1),
    }


def build(nc, t, o):
    ctx = ExitStack()
    base = 16512
    placed = {}

    def at(name, shape, dt, off):
        placed[name] = off
        return nc.alloc_sbuf_tensor_at(name, shape, dt, offset=base + off)

    raw = at("raw", [P, RING, CK, CW], F32, 0)
    wH = at("wH", [P, RING, CK, CW], F32R, 16384)
    wL = at("wL", [P, RING, CK, CW], F32R, 32768)
    xr = at("xr", [P, KT, N], F32, 49152)
    M0 = 66048
    hH = at("hH", [P, FT, N], F32R, M0)
    hL = at("hL", [P, FT, N], F32R, M0 + 46464)
    xH = at("xH", [P, KT, N], F32R, M0 + 92928)
    xL = at("xL", [P, KT, N], F32R, M0 + 109824)
    E0 = M0 + 126720
    gt = at("gt", [P, 2, N], F32, E0)
    st = at("st", [P, 2, N], F32, E0 + 2112)
    ut = at("ut", [P, 2, N], F32, E0 + 4224)
    hf = at("hf", [P, 2, N], F32, E0 + 6336)
    sq = at("sq", [P, 2, 2, N], F32, E0 + 8448)
    acc = at("acc", [P, 2, N], F32, E0 + 12672)
    K0 = E0 + 14784
    rs = at("rs", [P, N], F32, K0)
    sd = at("sd", [P, N], F32, K0 + 1056)
    vcol = at("vcol", [P, 2, 68], F32, K0 + 2112)
    cb = at("cb", [P, 2 * P], F32, K0 + 2656)
    ones = at("ones", [P, P], F32, K0 + 3680)
    eps = at("eps", [P, 4], F32, K0 + 4192)
    vrowb = at("vrowb", [68, P], F32, K0 + 4224)
    ident, blk = cb[:, 0:P], cb[:, P:2 * P]
    ep, gep = eps[:, 0:1], eps[:, 1:2]

    xin = at("xin", [P, 2, D], F32, M0)
    xsin = at("xsin", [NB, D], F32, M0 + 16384)
    vrowa = at("vrowa", [68, P], F32, M0 + 24576)
    yst = at("yst", [P, 2, 2, CW], F32, M0 + 92928)
    yss = at("yss", [NB, 2, CW], F32, M0 + 92928 + 4096)
    yf = at("yf", [P, 2, 2, N], F32, M0 + 92928 + 6144)

    mixH = at("mixH", [P, KT, N], F32R, M0)
    mixL = at("mixL", [P, KT, N], F32R, M0 + 16896)
    PB = M0 + 33792
    pj = at("pj", [P, MT, N], F32, PB)
    Q0 = PB + 52800
    crow = at("crow", [16, RW], F32, Q0)
    srow = at("srow", [NB, 20 * P], F32, Q0 + 3072)
    zc = at("zc", [P, RT, T + 2], F32, Q0 + 13312)
    yc = at("yc", [P, RT, N], F32, Q0 + 19520)
    zs = at("zs", [P, RT, 3, NB], F32, Q0 + 25856)
    zo = at("zo", [P, 10, RT], F32, Q0 + 26432)
    zoT = at("zoT", [60, P], F32, E0 + 6144)
    ctmp = at("ctmp", [P, RT, NB], F32, Q0 + 27168)
    so = at("so", [P, 2, P], F32, E0 + 6656)
    kv = at("kv", [P, 4, 512], F32, Q0)
    catt = at("catt", [P, 768], F32, Q0 + 8192)
    sc = at("sc", [P, 8, 384], F32, Q0 + 11264)
    rq = at("rq", [P, 8, N], F32, Q0 + 23552)
    qkr = at("qkr", [96, P], F32, Q0 + 32000)
    kb = at("kb", [P, 2, 3, 512], F32, Q0)
    vb = at("vb", [P, 2, 3, 512], F32, Q0 + 12288)
    prod = at("prod", [P, 3, 512], F32, Q0 + 24576)
    qb = at("qb", [P, 2, 512], F32, Q0 + 32768)
    ss = at("ss", [P, 3, 2, NB, 4], F32, Q0 + 36864)
    pS = at("pS", [P, 3, 2, 32], F32, Q0 + 37632)
    osm = at("osm", [P, 64], F32, Q0 + 38400)
    sa = at("sa", [32, 2, 385], F32, E0 + 8448)
    calb = at("calb", [32, 768], F32, E0 + 11552)
    pex = at("pex", [32, 2, 64], F32, E0 + 5632)
    psf = at("psf", [P, 32], F32, E0 + 5504)
    shc = at("shc", [P, 180], F32, E0 + 4224)
    qkc = at("qkc", [P, 96], F32, E0 + 4960)
    shT = at("shT", [P, 20, NB], F32, E0)
    ST = at("ST", [P, RT, C], F32, E0 + 640)
    wc = at("wc", [P, RT, 4], F32, E0 + 2176)
    am = at("am", [P, 64], F32, E0 + 2272)
    svec = at("svec", [P, 6, 48], F32, E0 + 2528)
    cgat = at("cgat", [96, 50], F32, E0 + 3680)
    smal = at("smal", [96, 66], F32, E0 + 3936)
    G = RT * N * 4
    PR = PB + 12 * N * 4
    aT = at("aT", [P, RT, N], F32, PB)
    bT = at("bT", [P, RT, N], F32, PB + G)
    F0 = PB + 32 * N * 4
    gg = at("gg", [P, RT, N], F32, F0)
    bv = at("bv", [P, RT, N], F32, F0 + G)
    L0 = F0 + 2 * G
    sw = at("sw", [P, RT, N], F32, L0)
    lc = at("lc", [P, RT, N], F32, L0 + G)
    aa = at("aa", [P, RT, N], F32, L0 + 2 * G)
    kk = at("kk", [P, RT, N], F32, L0 + 3 * G)
    t1 = at("t1", [P, RT, N], F32, L0 + 4 * G)
    t2 = at("t2", [P, RT, N], F32, L0 + 5 * G)
    lora = at("lora", [P, 2, RW], F32, L0 + 6 * G)
    dif = at("dif", [P, 20, N], F32, L0)
    rst = at("rst", [P, T], F32, E0 + 12544)
    S1 = at("S1", [96, C, C], F32, L0)
    S2 = at("S2", [96, C, C], F32, L0 + 16384)
    sT = at("sT", [96, 3, P], F32, L0 + 32768)
    sv = at("sv", [96, 6, C], F32, L0 + 34304)
    ycat = at("ycat", [96, 2, C], F32, L0 + 35840)
    cm = at("cm", [P, 16, C], F32, E0 + 8448)
    Abd = at("Abd", [P, H, P], F32, L0)
    Xbd = at("Xbd", [P, H, P], F32, L0 + 6144)
    Qbd = at("Qbd", [P, H, P], F32, L0 + 12288)
    Zc = at("Zc", [P, H, C], F32, L0 + 18432)
    Xc = at("Xc", [P, H, C], F32, L0 + 21504)
    Qc = at("Qc", [P, H, C], F32, L0 + 24576)
    Aak = at("Aak", [P, H, C], F32, L0 + 27648)
    Arb = at("Arb", [P, H, C], F32, L0 + 30720)
    Ark = at("Ark", [P, H, C], F32, L0 + 33792)
    tok = at("tok", [P, 3, RW], F32, L0 + 36864)
    assert L0 + 36864 + 9216 <= E0
    Fc, Uc = Qc, Xc
    wkT = at("wkT", [C, RT, P], F32, L0)
    assert base + K0 + 4736 <= 229344

    ps = ctx.enter_context(nc.psum_tensor("ps", [P, 8, 512], F32))
    sems = {}

    def S(name):
        if name not in sems:
            sems[name] = ctx.enter_context(nc.semaphore(name))
        return sems[name]

    q_dram = nc.dram_tensor("q_rows", (NB, 512), F32, kind="Internal").ap()
    s_dram = nc.dram_tensor("wkv_rows", (6 * 48, P), F32, kind="Internal").ap()

    block = ctx.enter_context(nc.Block())

    def w_view(name):
        return t[name][0].rearrange("(kt p) f -> p kt f", p=P)

    views = {n: w_view(n) for n in ("ffn1_w_gate", "ffn1_w_up", "ffn1_w_down", "w_in", "w_out",
                                    "ffn2_w_gate", "ffn2_w_up", "ffn2_w_down")}

    def number(first, per, i, k):
        return i * per + (first + k)

    def load(sp, view, k0, nk, pair, first, per, i, k, fresh=False):
        if not fresh:
            sp.wait_ge(S("tail_made"), number(first, per, i, k) - RING + 1)
        sp.dma_start(raw[:, k % RING, 0:nk, :], view[:, k0:k0 + nk, bass.ds(pair * CW, CW)]
                     ).then_inc(S(f"landed{k % RING}"), 16)

    def head(act, nk, first, per, i, k, fresh=False):
        act.wait_ge(S(f"landed{k % RING}"), i * (16 * (per // RING)) + 16 * (first // RING + k // RING + 1))
        if not fresh:
            act.wait_ge(S("chunk_used"), number(first, per, i, k) - RING + 1)
        nc.scalar.activation(wH[:, k % RING, 0:nk, :], raw[:, k % RING, 0:nk, :], ACT.Copy
                             ).then_inc(S("head_made"), 1)

    def tail(dve, nk, first, per, i, k):
        dve.wait_ge(S("head_made"), number(first, per, i, k) + 1)
        nc.vector.tensor_tensor(wL[:, k % RING, 0:nk, :], raw[:, k % RING, 0:nk, :],
                                wH[:, k % RING, 0:nk, :].bitcast(F32), ALU.subtract
                                ).then_inc(S("tail_made"), 1)

    def products(pe, vH, vL, k0, nk, bank, start, stop, first, per, i, k):
        pe.wait_ge(S("tail_made"), number(first, per, i, k) + 1)
        for q in range(nk):
            for half in range(2):
                cols = slice(half * P, half * P + P)
                out = ps[:, bank + half, 0:N]
                a, b = start and q == 0, stop and q == nk - 1
                nc.tensor.matmul(out, wH[:, k % RING, q, cols], vH[:, k0 + q, :], start=a, stop=False)
                nc.tensor.matmul(out, wH[:, k % RING, q, cols], vL[:, k0 + q, :], start=False, stop=False)
                last = nc.tensor.matmul(out, wL[:, k % RING, q, cols], vH[:, k0 + q, :], start=False, stop=b)
        last.then_inc(S("chunk_used"), 1)

    def two(ap):
        return ap[:].unsqueeze(1).broadcast_to([P, 2, N])


    def early(q):
        return isinstance(q, int) and q < 2

    def squares_and_heads(act, w, q, slot):
        act.wait_ge(S("x_ready"), 8 * w + 1 + q)
        if w or not early(q):
            act.wait_ge(S("squares_added"), 8 * w - 1 + q)
        nc.scalar.activation(sq[:, slot, :, :], xr[:, bass.ds(q * 2, 2), :], ACT.Square
                             ).then_inc(S("squares_made"), 1)
        for e in range(2):
            nc.scalar.activation(xH[:, bass.ds(q * 2 + e, 1), :], xr[:, bass.ds(q * 2 + e, 1), :], ACT.Copy,
                                 scale=vcol[:, 0, bass.ds(q * 2 + (16 * w + e), 1)]
                                 ).then_inc(S("x_head"), 1)

    def x_tails(dve, w, q):
        dve.wait_ge(S("x_head"), 16 * w + 2 + q * 2)
        for e in range(2):
            nc.vector.scalar_tensor_tensor(
                xL[:, bass.ds(q * 2 + e, 1), :], xr[:, bass.ds(q * 2 + e, 1), :],
                vcol[:, 0, bass.ds(q * 2 + (16 * w + e), 1)],
                xH[:, bass.ds(q * 2 + e, 1), :].bitcast(F32), ALU.mult, ALU.subtract
            ).then_inc(S("x_tail"), 1)

    def x_add(dve, w, q, bank, factor, used):
        dve.wait_ge(S("chunk_used"), used)
        nc.vector.scalar_tensor_tensor(xr[:, bass.ds(q * 2, 2), :], ps[:, bank:bank + 2, 0:N], factor,
                                       xr[:, bass.ds(q * 2, 2), :], ALU.mult, ALU.add
                                       ).then_inc(S("x_ready"), 1)

    def norm_sum(pe, w):
        pe.wait_ge(S("squares_added"), 8 * w + 8)
        if w == 0:
            pe.wait_ge(S("constants_set"), 3)
        nc.tensor.matmul(ps[:, 4, 0:N], ones[:], acc[:, 0, :], start=True, stop=False)
        nc.tensor.matmul(ps[:, 4, 0:N], ones[:], acc[:, 1, :], start=False, stop=True
                         ).then_inc(S("norm_summed"), 1)

    def norm_root(act, w):
        act.wait_ge(S("norm_summed"), w + 1)
        nc.scalar.activation(sd[:], ps[:, 4, 0:N], ACT.Sqrt, bias=ep, scale=1.0 / D
                             ).then_inc(S("norm_root"), 1)

    def norm_reciprocal(dve, w):
        dve.wait_ge(S("norm_root"), w + 1)
        nc.vector.reciprocal(rs[:], sd[:]).then_inc(S("norm_ready"), 1)
        dve.wait_ge(S("norm_ready"), w + 1)

    def gate_scale(dve, u, first, p):
        dve.wait_ge(S("chunk_used"), first + 4 + p * GU_PER)
        nc.vector.tensor_tensor(gt[:], ps[:, 0:2, 0:N], two(rs), ALU.mult).then_inc(S("gate_scaled"), 1)

    def gate_silu(act, u, p):
        act.wait_ge(S("gate_scaled"), FT // 2 * u + 1 + p)
        nc.scalar.activation(st[:], gt[:], ACT.Silu).then_inc(S("silu_made"), 1)

    def hidden(dve, u, first, p):
        dve.wait_ge(S("chunk_used"), first + GU_PER + p * GU_PER)
        nc.vector.tensor_tensor(ut[:], ps[:, 2:4, 0:N], two(rs), ALU.mult).then_inc(S("up_scaled"), 1)
        dve.wait_ge(S("up_scaled"), FT // 2 * u + 1 + p)
        dve.wait_ge(S("silu_made"), FT // 2 * u + 1 + p)
        nc.vector.tensor_tensor(hf[:], st[:], ut[:], ALU.mult).then_inc(S("hidden_made"), 1)

    def hidden_head(act, u, p):
        act.wait_ge(S("hidden_made"), FT // 2 * u + 1 + p)
        nc.scalar.activation(hH[:, bass.ds(p * 2, 2), :], hf[:], ACT.Copy).then_inc(S("hidden_head"), 1)

    def hidden_tail(dve, u, p):
        dve.wait_ge(S("hidden_head"), FT // 2 * u + 1 + p)
        nc.vector.tensor_tensor(hL[:, bass.ds(p * 2, 2), :], hf[:], hH[:, bass.ds(p * 2, 2), :].bitcast(F32),
                                ALU.subtract).then_inc(S("hidden_tail"), 1)

    FFN = ((0, GU1, DN1, "ffn1"), (1, GU2, DN2, "ffn2"))

    def sp_ffn(sp, u, gu, dn, name):
        def step(i, fresh=False):
            for k in range(GU_PER):
                load(sp, views[name + ("_w_gate" if k < 4 else "_w_up")], CK * (k % 4), CK, i, gu, GU_PER, i, k,
                     fresh=fresh and k < RING)
        step(0, fresh=u == 0)
        with sp.Fori(1, FT // 2) as i:
            step(i)
        with sp.Fori(0, KT // 2) as i:
            for k in range(DN_PER):
                load(sp, views[name + "_w_down"], DN_K0[k], DN_KT[k], i, dn, DN_PER, i, k)

    def sp_square(sp, name, pairs, first):
        with sp.Fori(0, pairs) as i:
            for k in range(4):
                load(sp, views[name], CK * k, CK, i, first, 4, i, k)

    def act_ffn(act, u, gu, dn):
        def gate_up(i, first_pair):
            for k in range(5):
                head(act, CK, gu, GU_PER, i, k, fresh=first_pair and u == 0 and k < RING)
            if not first_pair:
                hidden_head(act, u, i - 1)
            elif u == 1:
                squares_and_heads(act, 2, KT // 2 - 1, 1)
            for k in range(5, GU_PER):
                head(act, CK, gu, GU_PER, i, k)
            if first_pair:
                norm_root(act, 2 * u)
            gate_silu(act, u, i)

        def down(i, jj, first_pair):
            q = i * 2 + jj
            for k in range(5):
                head(act, DN_KT[k], dn + DN_PER * jj, 2 * DN_PER, i, k)
            if first_pair:
                hidden_head(act, u, FT // 2 - 1)
            elif u == 0:
                squares_and_heads(act, 1, q - 1, 1 - jj)
            for k in range(5, 8):
                head(act, DN_KT[k], dn + DN_PER * jj, 2 * DN_PER, i, k)
            if u == 1 and not first_pair:
                stage_y(act, q - 1, 1 - jj)
            for k in range(8, DN_PER):
                head(act, DN_KT[k], dn + DN_PER * jj, 2 * DN_PER, i, k)

        gate_up(0, True)
        with act.Fori(1, FT // 2) as i:
            gate_up(i, False)
        for jj in range(2):
            down(0, jj, jj == 0)
        for jj in range(2 * u):
            down(1, jj, False)
        with act.Fori(1 + u, KT // 4) as i:
            for jj in range(2):
                down(i, jj, False)
        if u == 1:
            stage_y(act, KT // 2 - 1, 1)

    def stage_y(act, q, slot):
        act.wait_ge(S("y_turned"), q + 1)
        if not early(q):
            act.wait_ge(S(f"y_out{slot}"), q * 16 - 16 * slot)
        nc.scalar.activation(yst[:, slot, :, :], ps[:, 2 * slot, :].rearrange("p (b c) -> p b c", b=2), ACT.Copy
                             ).then_inc(S("y_staged"), 1)
        nc.scalar.activation(yss[:, slot, :], ps[0:NB, 2 * slot + 1, 0:CW], ACT.Copy).then_inc(S("y_staged"), 1)

    def act_in(act):
        for k in range(4):
            head(act, CK, IN, IN_PER, 0, k)
        squares_and_heads(act, 1, KT // 2 - 1, 1)
        for k in range(4):
            head(act, CK, IN + 4, IN_PER, 0, k)
        norm_root(act, 1)
        for k in range(4):
            head(act, CK, IN + 8, IN_PER, 0, k)
        with act.Fori(3, MT // 2) as i:
            for k in range(4):
                head(act, CK, IN, IN_PER, i, k)

    def act_out(act):
        def pair(i, jj):
            for k in range(4):
                head(act, CK, OUT + 4 * jj, 8, i, k)
            squares_and_heads(act, 2, i * 2 + (jj - 1), 1 - jj)
        pair(0, 1)
        with act.Fori(1, KT // 4) as i:
            for jj in range(2):
                pair(i, jj)

    def dve_ffn(dve, u, gu, dn):
        def gate_up(i, first_pair):
            for k in range(4):
                tail(dve, CK, gu, GU_PER, i, k)
            if not first_pair:
                hidden(dve, u, gu, i - 1)
            elif u == 1:
                x_add(dve, 2, KT // 2 - 1, 6, 1.0, GU2)
            tail(dve, CK, gu, GU_PER, i, 4)
            if not first_pair:
                hidden_tail(dve, u, i - 1)
            elif u == 1:
                x_tails(dve, 2, KT // 2 - 1)
            for k in range(5, GU_PER):
                tail(dve, CK, gu, GU_PER, i, k)
            if first_pair:
                norm_reciprocal(dve, 2 * u)
            gate_scale(dve, u, gu, i)

        def down(i, jj, first_pair):
            q = i * 2 + jj
            for k in range(4):
                tail(dve, DN_KT[k], dn + DN_PER * jj, 2 * DN_PER, i, k)
            if first_pair:
                hidden(dve, u, gu, FT // 2 - 1)
            elif u == 0:
                x_add(dve, 1, q - 1, 6 - 2 * jj, 0.5, q * DN_PER + dn)
            else:
                y_add(dve, q - 1, 1 - jj, q * DN_PER + dn)
            tail(dve, DN_KT[4], dn + DN_PER * jj, 2 * DN_PER, i, 4)
            if first_pair:
                hidden_tail(dve, u, FT // 2 - 1)
            elif u == 0:
                x_tails(dve, 1, q - 1)
            for k in range(5, DN_PER):
                tail(dve, DN_KT[k], dn + DN_PER * jj, 2 * DN_PER, i, k)

        gate_up(0, True)
        with dve.Fori(1, FT // 2) as i:
            gate_up(i, False)
        for jj in range(2):
            down(0, jj, jj == 0)
        for jj in range(2 * u):
            down(1, jj, False)
        with dve.Fori(1 + u, KT // 4) as i:
            for jj in range(2):
                down(i, jj, False)
        if u == 1:
            y_add(dve, KT // 2 - 1, 1, dn + DN_PER * KT // 2)

    def y_add(dve, q, slot, used):
        dve.wait_ge(S("chunk_used"), used)
        if not early(q):
            dve.wait_ge(S("y_turned"), q - 1)
        nc.vector.scalar_tensor_tensor(yf[:, slot, :, :], ps[:, 4 + 2 * slot:6 + 2 * slot, 0:N], 0.5,
                                       xr[:, bass.ds(q * 2, 2), :], ALU.mult, ALU.add
                                       ).then_inc(S("x_ready"), 1)

    def project(dve, q, bank):
        dve.wait_ge(S("chunk_used"), IN + IN_PER + q * IN_PER)
        nc.vector.tensor_tensor(pj[:, bass.ds(q * 2, 2), :], ps[:, bank:bank + 2, 0:N], two(rs), ALU.mult
                                ).then_inc(S("projected"), 1)

    def dve_in(dve):
        for k in range(4):
            tail(dve, CK, IN, IN_PER, 0, k)
        x_add(dve, 1, KT // 2 - 1, 6, 0.5, IN)
        x_tails(dve, 1, KT // 2 - 1)
        for k in range(4):
            tail(dve, CK, IN + 4, IN_PER, 0, k)
        norm_reciprocal(dve, 1)
        project(dve, 0, 0)
        for k in range(4):
            tail(dve, CK, IN + 8, IN_PER, 0, k)
        project(dve, 1, 2)
        with dve.Fori(0, (MT // 2 - 3) // 2) as i:
            for jj in range(2):
                for k in range(4):
                    tail(dve, CK, IN + 12 + 4 * jj, 8, i, k)
                project(dve, i * 2 + (2 + jj), 2 * jj)

    def dve_out(dve):
        def pair(i, jj):
            for k in range(4):
                tail(dve, CK, OUT + 4 * jj, 8, i, k)
            x_add(dve, 2, i * 2 + (jj - 1), 6 - 2 * jj, 1.0, OUT + 4 * jj + i * 8)
            x_tails(dve, 2, i * 2 + (jj - 1))
        pair(0, 1)
        with dve.Fori(1, KT // 4) as i:
            for jj in range(2):
                pair(i, jj)

    def pe_ffn(pe, u, gu, dn):
        w = 2 * u

        def gate_up(i, first_pair):
            for k in range(GU_PER):
                if first_pair and k < 4:
                    pe.wait_ge(S("x_tail"), 16 * w + 4 * (k + 1))
                if k == 0 and not first_pair:
                    pe.wait_ge(S("gate_scaled"), FT // 2 * u + i)
                if k == 4 and not first_pair:
                    pe.wait_ge(S("up_scaled"), FT // 2 * u + i)
                products(pe, xH, xL, CK * (k % 4), CK, 0 if k < 4 else 2, k % 4 == 0, k % 4 == 3,
                         gu, GU_PER, i, k)
                if k == 3 and first_pair:
                    norm_sum(pe, w)

        def down(i, jj, first_pair):
            q = i * 2 + jj
            if not (isinstance(i, int) and i == 0):
                pe.wait_ge(S("x_ready"), 8 * (w + 1) - 1 + q)
            for k in range(DN_PER):
                if first_pair:
                    pe.wait_ge(S("hidden_tail"), FT // 2 * u + (DN_K0[k] + DN_KT[k] + 1) // 2)
                products(pe, hH, hL, DN_K0[k], DN_KT[k], 4 + 2 * jj, k == 0, k == DN_PER - 1,
                         dn + DN_PER * jj, 2 * DN_PER, i, k)
                if u == 1 and not first_pair and k == 5:
                    turn_y(pe, q - 1, 1 - jj)

        gate_up(0, True)
        with pe.Fori(1, FT // 2) as i:
            gate_up(i, False)
        for jj in range(2):
            down(0, jj, jj == 0)
        for jj in range(2 * u):
            down(1, jj, False)
        with pe.Fori(1 + u, KT // 4) as i:
            for jj in range(2):
                down(i, jj, False)
        if u == 1:
            turn_y(pe, KT // 2 - 1, 1)

    def turn_y(pe, q, slot):
        pe.wait_ge(S("x_ready"), 25 + q)
        if not early(q):
            pe.wait_ge(S("y_staged"), q * 2 - 2)
        for e in range(2):
            for b in range(2):
                nc.tensor.transpose(ps[:, 2 * slot, b * CW + e * P:b * CW + e * P + P],
                                    yf[:, slot, e, b * P:b * P + P], ident)
            last = nc.tensor.transpose(ps[0:NB, 2 * slot + 1, e * P:e * P + P], yf[:, slot, e, T:N], ident)
        last.then_inc(S("y_turned"), 1)

    def pe_in(pe):
        for k in range(4):
            pe.wait_ge(S("x_tail"), 16 + 4 * (k + 1))
            products(pe, xH, xL, CK * k, CK, 0, k == 0, k == 3, IN, IN_PER, 0, k)
        norm_sum(pe, 1)
        for k in range(4):
            products(pe, xH, xL, CK * k, CK, 2, k == 0, k == 3, IN + 4, IN_PER, 0, k)
        for k in range(4):
            if k == 0:
                pe.wait_ge(S("projected"), 1)
            products(pe, xH, xL, CK * k, CK, 0, k == 0, k == 3, IN + 8, IN_PER, 0, k)
        with pe.Fori(0, (MT // 2 - 3) // 2) as i:
            for jj in range(2):
                pe.wait_ge(S("projected"), 2 + jj + i * 2)
                for k in range(4):
                    products(pe, xH, xL, CK * k, CK, 2 - 2 * jj, k == 0, k == 3, IN + 12 + 4 * jj, 8, i, k)

    def pe_out(pe):
        def pair(i, jj):
            if not (isinstance(i, int) and i == 0):
                pe.wait_ge(S("x_ready"), 15 + jj + i * 2)
            for k in range(4):
                products(pe, mixH, mixL, CK * k, CK, 4 + 2 * jj, k == 0, k == 3, OUT + 4 * jj, 8, i, k)
        for jj in range(2):
            pair(0, jj)
        with pe.Fori(1, KT // 4) as i:
            for jj in range(2):
                pair(i, jj)

    def pool_squares(pool, w):
        def add(q, slot):
            pool.wait_ge(S("squares_made"), 8 * w + 1 + q)
            pool.wait_ge(S("squares_added"), 8 * w + q)
            nc.gpsimd.tensor_tensor(acc[:], acc[:], sq[:, slot, :, :], ALU.add).then_inc(S("squares_added"), 1)
        pool.wait_ge(S("squares_made"), 8 * w + 1)
        nc.gpsimd.tensor_copy(acc[:], sq[:, 0, :, :]).then_inc(S("squares_added"), 1)
        add(1, 1)
        with pool.Fori(1, 4) as i:
            for jj in range(2):
                add(i * 2 + jj, jj)

    def pool_y(pool):
        yp = o[0][0].rearrange("(b p) f -> p b f", p=P)
        ys = o[1].rearrange("b s f -> (b s) f")
        with pool.Fori(0, KT // 4) as i:
            for jj in range(2):
                pool.wait_ge(S("y_staged"), 2 + 2 * jj + i * 4)
                pool.dma_start(yp[:, :, bass.ds(i * (2 * CW) + jj * CW, CW)], yst[:, jj, :, :]
                               ).then_inc(S(f"y_out{jj}"), 16)
                pool.dma_start(ys[:, bass.ds(i * (2 * CW) + jj * CW, CW)], yss[:, jj, :]
                               ).then_inc(S(f"y_out{jj}"), 16)
        for jj in range(2):
            pool.wait_ge(S(f"y_out{jj}"), 32 * (KT // 4))

    def row_view(name, width=None):
        return t[name][0].rearrange("(r c) -> r c", c=P)

    def act_start(act):
        act.dma_start(cb[:], t["c_base"]).then_inc(S("base_in"), 16)
        act.dma_start(xsin[:], t["x_sample"].rearrange("b s f -> (b s) f")).then_inc(S("x_in"), 16)
        for name, r, n in (("ffn1_norm", "ffn1", 16), ("mix_norm", "mix", 16), ("ffn2_norm", "ffn2", 16),
                           ("rwkv_mu", "mu", 20)):
            act.dma_start(vrowa[VA[r]:VA[r] + n, :], row_view(name)).then_inc(S("vectors_a_in"), 16)
        act.wait_ge(S("vectors_a_set"), 1)
        for q in range(KT // 2):
            squares_and_heads(act, 0, q, q % 2)

    def sp_start(sp):
        xp = t["x_prompt"][0].rearrange("(b p) f -> p b f", p=P)
        sp.dma_start(xin[:], xp).then_inc(S("x_in"), 16)

    def pool_start(pool):
        nc.gpsimd.memset(ones[:], 1.0).then_inc(S("constants_set"), 1)
        nc.gpsimd.memset(ep, EPS).then_inc(S("constants_set"), 1)
        nc.gpsimd.memset(gep, GN_EPS).then_inc(S("constants_set"), 1)
        n = 0
        for name, r in (("rwkv_w0", "w0"), ("rwkv_a0", "a0"), ("rwkv_k_k", "kk"), ("rwkv_k_a", "ka"),
                        ("rwkv_ln_w", "lnw"), ("rwkv_ln_b", "lnb"), ("conv_b", "cb")):
            pool.dma_start(vrowb[VB[r]:VB[r] + RT, :], row_view(name)).then_inc(S("vectors_b_in"), 16)
        pool.dma_start(vrowb[VB["rk"]:VB["rk"] + RT, :], t["rwkv_r_k"][0].rearrange("(r a) c -> r (a c)", a=2)
                       ).then_inc(S("vectors_b_in"), 16)
        pool.dma_start(vrowb[VB["cw"]:VB["cw"] + 3 * RT, :], t["conv_w"][0].rearrange("i (r c) -> (i r) c", c=P)
                       ).then_inc(S("vectors_b_in"), 16)
        for name, r in (("q_norm", "qn"), ("k_norm", "kn")):
            for a in range(2):
                pool.dma_start(vrowb[VB[r]:VB[r] + 1, a * C:a * C + C], t[name]).then_inc(S("vectors_b_in"), 16)

    def pe_start(pe):
        pe.wait_ge(S("base_in"), 16)
        pe.wait_ge(S("vectors_a_in"), 64)
        nc.tensor.transpose(ps[:, 0, 0:68], vrowa[:], ident[0:68, 0:68]).then_inc(S("vectors_a_turned"), 1)
        pe.wait_ge(S("x_in"), 32)
        for q in range(KT // 2):
            if q >= 2:
                pe.wait_ge(S("x_ready"), q - 1)
            for d in (2 * q, 2 * q + 1):
                for b in range(2):
                    nc.tensor.transpose(ps[:, 4 + d % 4, b * P:b * P + P], xin[:, b, d * P:d * P + P], ident)
                last = nc.tensor.transpose(ps[:, 4 + d % 4, T:N], xsin[:, d * P:d * P + P], ident[0:NB, 0:NB])
            last.then_inc(S("x_turned"), 1)

    def dve_start(dve):
        dve.wait_ge(S("vectors_a_turned"), 1)
        nc.vector.tensor_copy(vcol[:, 0, :], ps[:, 0, 0:68]).then_inc(S("vectors_a_set"), 1)
        dve.wait_ge(S("vectors_a_set"), 1)
        for q in range(KT // 2 + 1):
            if q < KT // 2:
                dve.wait_ge(S("x_turned"), q + 1)
                b = 4 + 2 * (q % 2)
                nc.vector.tensor_copy(xr[:, 2 * q:2 * q + 2, :], ps[:, b:b + 2, 0:N]).then_inc(S("x_ready"), 1)
            if q >= 1:
                x_tails(dve, 0, q - 1)

    pu, pb, pc = pj[:, 32:38], pj[:, 38:44], pj[:, 44:50]

    def vec(name, j=0, n=1):
        return vcol[:, 1, VB[name] + j:VB[name] + j + n]

    def spread(ap, n):
        return ap.unsqueeze(2).broadcast_to([P, ap.shape[1], n])

    chain = [0]

    def link(ins, dve):
        chain[0] += 1
        ins.then_inc(S("vector_step"), 1)
        dve.wait_ge(S("vector_step"), chain[0])

    def linked(instrs, dve):
        for ins in instrs:
            chain[0] += 1
            ins.then_inc(S("vector_step"), 1)
        dve.wait_ge(S("vector_step"), chain[0])

    def pool_shift_conv(pool):
        pool.wait_ge(S("projected"), MT // 2)
        pool.dma_start(crow[:], t["state_conv"][0].rearrange("b i f -> (b i) f")).then_inc(S("rows_in"), 16)
        pool.dma_start(srow[:], t["state_shift"][0]).then_inc(S("rows_in"), 16)
        pool.dma_start(o[11][0, :, 0, :], t["state_conv"][0][:, 1, :]).then_inc(S("written"), 16)
        pool.wait_ge(S("state_rows"), 3)
        pool.dma_start(o[5][0].rearrange("a (r c) -> (a r) c", c=P), so[0:20, 0, :]).then_inc(S("written"), 16)
        shift = o[10][0].rearrange("b (r c) -> (b r) c", c=P)
        pool.dma_start(shift[0:100, :], so[20:120, 0, :]).then_inc(S("written"), 16)
        pool.dma_start(shift[100:160, :], so[0:60, 1, :]).then_inc(S("written"), 16)
        pool.dma_start(o[6][0, 0].rearrange("i (r c) -> (i r) c", c=P), zoT[0:12, :]).then_inc(S("written"), 16)
        for b in range(NB):
            pool.dma_start(o[11][0, b, 1, :].rearrange("(r c) -> r c", c=P), zoT[12 + 6 * b:18 + 6 * b, :]
                           ).then_inc(S("written"), 16)

    def pe_shift_conv(pe):
        pe.wait_ge(S("rows_in"), 32)
        pe.wait_ge(S("vectors_b_in"), 16 * 13)
        for j in range(RT):
            nc.tensor.transpose(ps[:, 0, j * 16:j * 16 + 16], crow[:, j * P:j * P + P], ident[0:16, 0:16])
        for j in range(20):
            nc.tensor.transpose(ps[:, 1, j * NB:j * NB + NB], srow[:, j * P:j * P + P], ident[0:NB, 0:NB])
        nc.tensor.transpose(ps[:, 2, 0:68], vrowb[:], ident[0:68, 0:68]).then_inc(S("rows_turned"), 1)
        pe.wait_ge(S("shift_columns"), 1)
        nc.tensor.transpose(ps[0:120, 4, 0:P], shc[:, 0:120], ident)
        nc.tensor.transpose(ps[0:60, 5, 0:P], shc[:, 120:180], ident).then_inc(S("shift_turned"), 1)
        pe.wait_ge(S("conv_state"), 2)
        nc.tensor.transpose(ps[0:60, 3, 0:P], zo[:].rearrange("p c r -> p (c r)"), ident
                            ).then_inc(S("conv_turned"), 1)

    def act_shift_conv(act):
        act.wait_ge(S("shift_turned"), 1)
        nc.scalar.activation(so[0:120, 0, :], ps[0:120, 4, 0:P], ACT.Copy).then_inc(S("state_rows"), 1)
        nc.scalar.activation(so[0:60, 1, :], ps[0:60, 5, 0:P], ACT.Copy).then_inc(S("state_rows"), 1)
        act.wait_ge(S("conv_turned"), 1)
        nc.scalar.activation(zoT[:], ps[0:60, 3, 0:P], ACT.Copy).then_inc(S("state_rows"), 1)
        act.wait_ge(S("conv_made"), 1)
        nc.scalar.activation(mixH[:, 10:16, :], yc[:], ACT.Copy).then_inc(S("conv_head"), 1)

    def dve_shift_conv(dve):
        dve.wait_ge(S("projected"), MT // 2)
        v = nc.vector
        v.tensor_copy(shc[:].rearrange("p (c r) -> p r c", r=20), pj[:, 12:32, T - 1:N]
                      ).then_inc(S("shift_columns"), 1)
        linked([
            v.memset(zc[:, :, 0:2], 0.0),
            v.tensor_tensor(zc[:, :, 2:T + 2], pc[:, :, 0:T], pu[:, :, 0:T], ALU.mult),
            v.tensor_tensor(zs[:, :, 2, :], pc[:, :, T:N], pu[:, :, T:N], ALU.mult),
        ], dve)
        v.tensor_copy(zo[:, 0:2, :].rearrange("p c r -> p r c"), zc[:, :, T:T + 2]).then_inc(S("conv_state"), 1)
        v.tensor_copy(zo[:, 2:10, :].rearrange("p c r -> p r c"), zs[:, :, 2, :]).then_inc(S("conv_state"), 1)
        dve.wait_ge(S("rows_turned"), 1)
        linked([
            v.tensor_copy(vcol[:, 1, :], ps[:, 2, 0:68]),
            v.tensor_copy(shT[:].rearrange("p r b -> p (r b)"), ps[:, 1, 0:160]),
            v.tensor_copy(zs[:, :, 0:2, :].rearrange("p r i b -> p r b i"),
                          ps[:, 0, 0:96].rearrange("p (r b i) -> p r b i", b=NB, i=2)),
        ], dve)
        for i in range(3):
            for j in range(RT):
                out, src = yc[:, j, 0:T], zc[:, j, i:i + T]
                if i == 0:
                    ins = v.tensor_scalar(out, src, vec("cw", j), vec("cb", j), ALU.mult, ALU.add)
                else:
                    ins = v.scalar_tensor_tensor(out, src, vec("cw", 6 * i + j), out, ALU.mult, ALU.add)
                chain[0] += 1
                ins.then_inc(S("vector_step"), 1)
            dve.wait_ge(S("vector_step"), chain[0])
        smp = yc[:, :, T:N]
        linked([v.tensor_tensor(smp, zs[:, :, 0, :], spread(vec("cw", 0, 6), NB), ALU.mult),
                v.tensor_tensor(ctmp[:], zs[:, :, 1, :], spread(vec("cw", 6, 6), NB), ALU.mult)], dve)
        link(v.tensor_tensor(smp, smp, ctmp[:], ALU.add), dve)
        link(v.tensor_tensor(ctmp[:], zs[:, :, 2, :], spread(vec("cw", 12, 6), NB), ALU.mult), dve)
        link(v.tensor_tensor(smp, smp, ctmp[:], ALU.add), dve)
        link(v.tensor_tensor(smp, smp, spread(vec("cb", 0, 6), NB), ALU.add), dve)
        v.tensor_tensor(yc[:], yc[:], pb, ALU.mult).then_inc(S("conv_made"), 1)
        dve.wait_ge(S("conv_head"), 1)
        v.tensor_tensor(mixL[:, 10:16, :], yc[:], mixH[:, 10:16, :].bitcast(F32), ALU.subtract
                        ).then_inc(S("conv_split"), 1)

    pq, pk, pv = pj[:, 0:4], pj[:, 4:8], pj[:, 8:12]

    def pe_attend_prompt(pe):
        pe.wait_ge(S("qk_squared"), 1)
        for j in range(8):
            last = nc.tensor.matmul(ps[:, j, 0:N], blk, rq[:, j, :], start=True, stop=True)
        last.then_inc(S("qk_summed"), 1)
        pe.wait_ge(S("qk_normed"), 2)
        for b in range(2):
            for j in range(4):
                nc.tensor.transpose(ps[:, b, j * P:j * P + P], pk[:, j, b * P:b * P + P], ident)
                nc.tensor.transpose(ps[:, 2 + b, j * P:j * P + P], pv[:, j, b * P:b * P + P], ident)
        pe.wait_ge(S("qkv_columns"), 1)
        nc.tensor.transpose(ps[0:96, 4, 0:P], qkc[:], ident).then_inc(S("qkv_turned"), 1)
        pe.wait_ge(S("qkv_rows"), 2)
        for h in range(8):
            f = slice(h % 2 * C, h % 2 * C + C)
            nc.tensor.matmul(ps[:, h, 0:P], pq[f, h // 2, 0:P], pk[f, h // 2, 0:P], start=True, stop=True)
            nc.tensor.matmul(ps[:, h, P:384], pq[f, h // 2, P:T], pk[f, h // 2, 0:T], start=True, stop=True
                             ).then_inc(S("scores_made"), 1)
        pe.wait_ge(S("probs_made"), 2)
        for h in range(8):
            for b in range(3):
                last = nc.tensor.transpose(ps[:, h, b * P:b * P + P], sc[:, h, b * P:b * P + P], ident)
            last.then_inc(S("probs_turned"), 1)
        pe.wait_ge(S("probs_v"), 4)
        pe.wait_ge(S("probs_a"), 4)
        for h in range(8):
            out = ps[h % 2 * C:h % 2 * C + C, h // 2, 0:T]
            d = slice(h * C, h * C + C)
            nc.tensor.matmul(out, kv[:, 2, d], sc[:, h, 0:T], start=True, stop=False)
            last = nc.tensor.matmul(out[:, P:T], kv[:, 3, d], sc[:, h, T:384], start=False, stop=True)
        last.then_inc(S("attended"), 1)

    def act_attend_prompt(act):
        act.wait_ge(S("conv_split"), 1)
        nc.scalar.activation(rq[:], pj[:, 0:8], ACT.Square).then_inc(S("qk_squared"), 1)
        act.wait_ge(S("qk_summed"), 1)
        nc.scalar.activation(rq[:], ps[:, :, 0:N], ACT.Sqrt, bias=ep, scale=1.0 / C).then_inc(S("qk_root"), 1)
        act.wait_ge(S("qkv_turned"), 1)
        nc.scalar.activation(kv[:], ps[:, 0:4, :], ACT.Copy).then_inc(S("qkv_rows"), 1)
        act.wait_ge(S("score_max"), 1)
        for b, cols in ((0, slice(0, P)), (1, slice(P, 384))):
            for h in range(8):
                nc.scalar.activation(sc[:, h, cols], sc[:, h, cols], ACT.Exp, bias=am[:, 16 + b * 8 + h:17 + b * 8 + h],
                                     scale=0.125).then_inc(S("exp_made"), 1)
        for h in range(4):
            act.wait_ge(S("probs_turned"), 2 * h + 2)
            nc.scalar.activation(sc[:, 2 * h + 1, :], ps[:, 2 * h + 1, 0:384], ACT.Copy).then_inc(S("probs_a"), 1)
        act.wait_ge(S("attended"), 1)
        nc.scalar.activation(mixH[:, 0:4, 0:T], ps[:, 0:4, 0:T], ACT.Copy).then_inc(S("attend_head"), 1)

    def dve_attend_prompt(dve):
        v = nc.vector
        dve.wait_ge(S("qk_root"), 1)
        link(v.reciprocal(rq[:], rq[:]), dve)
        v.scalar_tensor_tensor(pq, pq, vec("qn"), rq[:, 0:4], ALU.mult, ALU.mult).then_inc(S("qk_normed"), 1)
        v.scalar_tensor_tensor(pk, pk, vec("kn"), rq[:, 4:8], ALU.mult, ALU.mult).then_inc(S("qk_normed"), 1)
        dve.wait_ge(S("qk_normed"), 2)
        v.tensor_copy(qkc[:].rearrange("p (r b) -> p r b", b=NB), pj[:, 0:12, T:N]).then_inc(S("qkv_columns"), 1)
        dve.wait_ge(S("qkv_turned"), 1)
        v.tensor_copy(qkr[:], ps[0:96, 4, 0:P]).then_inc(S("qkv_rows"), 1)
        dve.wait_ge(S("att_tables_in"), 16)
        for h in range(8):
            dve.wait_ge(S("scores_made"), h + 1)
            chain[0] += 1
            v.scalar_tensor_tensor(sc[:, h, :], catt[:, 0:384], -8.0 * slope(h), ps[:, h, 0:384],
                                   ALU.mult, ALU.add).then_inc(S("vector_step"), 1)
        dve.wait_ge(S("vector_step"), chain[0])
        linked([v.tensor_reduce(am[:, 0:8], sc[:, :, 0:P], AX.X, ALU.max),
                v.tensor_reduce(am[:, 8:16], sc[:, :, P:384], AX.X, ALU.max)], dve)
        v.tensor_scalar(am[:, 16:32], am[:, 0:16], -0.125, None, ALU.mult).then_inc(S("score_max"), 1)
        dve.wait_ge(S("exp_made"), 16)
        mult = catt[:, 384:768].unsqueeze(1).broadcast_to([P, 8, 384])
        link(v.tensor_tensor(sc[:], sc[:], mult, ALU.mult), dve)
        linked([v.tensor_reduce(am[:, 32:40], sc[:, :, 0:P], AX.X, ALU.add),
                v.tensor_reduce(am[:, 40:48], sc[:, :, P:384], AX.X, ALU.add)], dve)
        link(v.reciprocal(am[:, 48:64], am[:, 32:48]), dve)
        v.tensor_tensor(sc[:, :, 0:P], sc[:, :, 0:P], spread(am[:, 48:56], P), ALU.mult).then_inc(S("probs_made"), 1)
        v.tensor_tensor(sc[:, :, P:384], sc[:, :, P:384], spread(am[:, 56:64], T), ALU.mult
                        ).then_inc(S("probs_made"), 1)
        for h in range(4):
            dve.wait_ge(S("probs_turned"), 2 * h + 1)
            v.tensor_copy(sc[:, 2 * h, :], ps[:, 2 * h, 0:384]).then_inc(S("probs_v"), 1)
        dve.wait_ge(S("attend_head"), 1)
        v.tensor_tensor(mixL[:, 0:4, 0:T], ps[:, 0:4, 0:T], mixH[:, 0:4, 0:T].bitcast(F32), ALU.subtract
                        ).then_inc(S("attend_split"), 1)

    def pool_attend_prompt(pool):
        pool.wait_ge(S("rows_turned"), 1)
        pool.dma_start(catt[:], t["c_att"]).then_inc(S("att_tables_in"), 16)
        pool.wait_ge(S("qkv_rows"), 2)
        for n, a in ((2, 0), (3, 2)):
            pool.dma_start(o[n][0, 0].rearrange("(b p) h e -> p b (h e)", p=P), kv[:, a:a + 2, :]
                           ).then_inc(S("prompt_kv_out"), 16)
        for n, r in ((7, 32), (8, 64)):
            for j in range(4):
                pool.dma_start(o[n][0, :, 0, 2 * j:2 * j + 2, :].rearrange("b h e -> b (h e)"),
                               qkr[r + 8 * j:r + 8 * j + 8, :]).then_inc(S("sample_kv_out"), 16)
        for j in range(4):
            pool.dma_start(q_dram[:, j * P:j * P + P], qkr[8 * j:8 * j + 8, :]).then_inc(S("sample_kv_out"), 16)
        pool.wait_ge(S("prompt_kv_out"), 32)
        pool.wait_ge(S("sample_kv_out"), 16 * 12)

    def pool_attend_sample(pool):
        pool.dma_start(calb[:], t["c_alibi"]).then_inc(S("alibi_in"), 16)
        pool.wait_ge(S("attended"), 1)
        pool.wait_ge(S("attend_split"), 1)

        def rows(cache, b, dst, s):
            src = t[cache][0, b].rearrange("s h e -> s (h e)")
            for g, dil in enumerate(DILATIONS):
                if dil == 1:
                    keys = src[PAST - P:PAST, :]
                else:
                    keys = src[PAST - dil * P:PAST, :].rearrange("(p d) f -> p d f", d=dil)[:, 0, :]
                pool.dma_start(dst[:, b % 2, g, :], keys).then_inc(S(f"{s}{b % 2}"), 16)
        for b in range(NB):
            if b >= 2:
                pool.wait_ge(S("key_scores"), b - 1)
            pool.dma_start(qb[:, b % 2, :], q_dram[b:b + 1, :].broadcast_to([P, 512])
                           ).then_inc(S(f"keys_in{b % 2}"), 16)
            rows("cache_swa_k", b, kb, "keys_in")
        for b in range(NB):
            if b >= 2:
                pool.wait_ge(S("values_used"), b - 1)
            rows("cache_swa_v", b, vb, "values_in")

    def dve_attend_sample(dve):
        v = nc.vector
        for b in range(NB):
            dve.wait_ge(S(f"keys_in{b % 2}"), 16 * 4 * (b // 2 + 1))
            if b:
                dve.wait_ge(S("key_scores"), b)
            q = qb[:, b % 2, :].unsqueeze(1).broadcast_to([P, 3, 512])
            link(v.tensor_tensor(prod[:], kb[:, b % 2, :, :], q, ALU.mult), dve)
            v.tensor_reduce(ss[:, :, :, b, :].rearrange("p g a j -> p g j a"),
                            prod[:].rearrange("p g (j a e) -> p g j a e", e=C, a=2), AX.X, ALU.add
                            ).then_inc(S("key_scores"), 1)
        v.tensor_tensor(psf[:].rearrange("p (b j) -> p j b", b=NB), pq[:, :, T:N], pk[:, :, T:N], ALU.mult
                        ).then_inc(S("self_product"), 1)
        dve.wait_ge(S("keys_turned"), 1)
        dve.wait_ge(S("alibi_in"), 16)
        linked([v.scalar_tensor_tensor(sa[:, :, 0:384], ps[0:32, 0:2, 0:384], 0.125,
                                       calb[:].rearrange("p (a k) -> p a k", a=2), ALU.mult, ALU.add),
                v.tensor_scalar(sa[:, :, 384], ps[0:32, 2, 0:2], 0.125, None, ALU.mult)], dve)
        link(v.tensor_reduce(smal[0:32, 0:2], sa[:], AX.X, ALU.max), dve)
        v.tensor_scalar(smal[0:32, 2:4], smal[0:32, 0:2], -1.0, None, ALU.mult).then_inc(S("sample_max"), 1)
        dve.wait_ge(S("sample_exp"), 2)
        link(v.tensor_scalar(sa[:, :, 384], sa[:, :, 384], 3.0, None, ALU.mult), dve)
        link(v.tensor_reduce(smal[0:32, 4:6], sa[:], AX.X, ALU.add), dve)
        link(v.reciprocal(smal[0:32, 6:8], smal[0:32, 4:6]), dve)
        for a in range(2):
            v.tensor_scalar(sa[:, a, :], sa[:, a, :], smal[0:32, 6 + a:7 + a], None, ALU.mult
                            ).then_inc(S("sample_probs"), 1)
        dve.wait_ge(S("sample_probs"), 2)
        v.tensor_copy(pex[:], sa[:, :, 384:385].broadcast_to([32, 2, C])).then_inc(S("self_probs"), 1)
        dve.wait_ge(S("sample_turned"), 1)
        v.tensor_copy(pS[:].rearrange("p g a m -> p (g a m)"), ps[:, 3, 0:192]).then_inc(S("sample_columns"), 1)
        dve.wait_ge(S("values_used"), NB)
        osf, oo = osm[:, 0:32], osm[:, 32:64]
        link(v.tensor_tensor(osf.rearrange("p (b j) -> p j b", b=NB),
                             ps[:, 5, 0:32].rearrange("p (b j) -> p j b", b=NB), pv[:, :, T:N], ALU.mult), dve)
        for a in range(2):
            f = slice(a * C, a * C + C)
            v.tensor_tensor(oo[f, :], ps[f, 4, 0:64].rearrange("p (m a) -> p m a", a=2)[:, :, a], osf[f, :], ALU.add
                            ).then_inc(S("sample_out"), 1)
        dve.wait_ge(S("sample_head"), 1)
        v.tensor_tensor(mixL[:, 0:4, T:N], oo.rearrange("p (b j) -> p j b", b=NB),
                        mixH[:, 0:4, T:N].bitcast(F32), ALU.subtract).then_inc(S("sample_split"), 1)

    def act_attend_sample(act):
        act.wait_ge(S("sample_max"), 1)
        for a in range(2):
            nc.scalar.activation(sa[:, a, :], sa[:, a, :], ACT.Exp, bias=smal[0:32, 2 + a:3 + a]
                                 ).then_inc(S("sample_exp"), 1)
        act.wait_ge(S("sample_out"), 2)
        nc.scalar.activation(mixH[:, 0:4, T:N], osm[:, 32:64].rearrange("p (b j) -> p j b", b=NB), ACT.Copy
                             ).then_inc(S("sample_head"), 1)

    def pe_attend_sample(pe):
        pe.wait_ge(S("attend_split"), 1)
        pe.wait_ge(S("key_scores"), NB)
        for a in range(2):
            for g in range(3):
                nc.tensor.transpose(ps[0:32, a, g * P:g * P + P], ss[:, g, a, :, :].rearrange("p b j -> p (b j)"), ident)
        pe.wait_ge(S("self_product"), 1)
        nc.tensor.matmul(ps[0:32, 2, 0:2], psf[:], blk[:, 0:P:C], start=True, stop=True
                         ).then_inc(S("keys_turned"), 1)
        pe.wait_ge(S("sample_probs"), 2)
        for g in range(3):
            for a in range(2):
                m = (2 * g + a) * 32
                last = nc.tensor.transpose(ps[:, 3, m:m + 32], sa[:, a, g * P:g * P + P], ident[0:32, 0:32])
        last.then_inc(S("sample_turned"), 1)
        pe.wait_ge(S("self_probs"), 1)
        nc.tensor.matmul(ps[:, 5, 0:32], pex[:].rearrange("p a e -> p (a e)"), ident[0:32, 0:32],
                         start=True, stop=True)
        pe.wait_ge(S("sample_columns"), 1)
        for b in range(NB):
            pe.wait_ge(S(f"values_in{b % 2}"), 48 * (b // 2 + 1))
            for j in range(4):
                m = 4 * b + j
                for g in range(3):
                    last = nc.tensor.matmul(ps[:, 4, 2 * m:2 * m + 2], vb[:, b % 2, g, j * P:j * P + P],
                                            pS[:, g, :, m], start=g == 0, stop=g == 2)
            last.then_inc(S("values_used"), 1)

    pr, pkr, pvr = pj[:, 12:18], pj[:, 18:24], pj[:, 24:30]
    px = pj[:, 12:32]
    pf = ps[:].rearrange("p b c -> p (b c)")

    def pool_rwkv(pool):
        pool.wait_ge(S("sample_split"), 1)
        pool.dma_start(lora[0:C, 0, :], t["rwkv_w2"][0]).then_inc(S("lora_in"), 16)
        pool.dma_start(lora[C:P, 0, :], t["rwkv_a2"][0]).then_inc(S("lora_in"), 16)
        pool.dma_start(lora[:, 1, :], t["rwkv_g2"][0]).then_inc(S("lora_in"), 16)
        pool.dma_start(cm[:], t["c_masks"].rearrange("p (m c) -> p m c", c=C)).then_inc(S("masks_in"), 16)
        pool.dma_start(cgat[:], t["c_gather"]).then_inc(S("gather_in"), 16)
        pool.wait_ge(S("decayed"), 4)
        pool.dma_start(S1[:], t["state_wkv"][0].rearrange("b h v k -> (b h) v k")).then_inc(S("state_in"), 16)
        pool.wait_ge(S("vectors_staged"), 1)
        pool.dma_start(s_dram.rearrange("(t p) c -> p t c", p=96), sT[:]).then_inc(S("vectors_out"), 16)
        pool.wait_ge(S("vectors_out"), 16)
        pool.dma_start(sv[:], s_dram.rearrange("(q m) (a e) -> (m a) q e", q=6, a=2)).then_inc(S("vectors_back"), 16)
        pool.wait_ge(S("sample_state"), 1)
        pool.dma_start(o[9][0].rearrange("b h v k -> (b h) v k"), S1[:]).then_inc(S("sample_state_out"), 16)
        pool.wait_ge(S("sample_state_out"), 16)
        pool.wait_ge(S("sample_turned_y"), 1)
        for m in (Abd, Xbd, Qbd):
            nc.gpsimd.memset(m[:], 0.0).then_inc(S("blocks_cleared"), 1)
        pool.wait_ge(S("final_state"), 1)
        for a in range(2):
            pool.dma_start(o[4][0, 0].rearrange("(j a) v k -> a v j k", a=2)[a], wkT[:, :, a * C:a * C + C]
                           ).then_inc(S("written"), 16)
        pool.wait_ge(S("written"), 16 * (5 + NB + 2))

    def pe_gates(pe):
        pe.wait_ge(S("lora_in"), 48)
        pe.wait_ge(S("lora_bent"), 2)
        for m in range(18):
            j = m % 6
            if m >= 8:
                pe.wait_ge(S("gates_out"), m - 7)
            cols = slice(j * P, j * P + P)
            if m < 6:
                a, b = lora[0:C, 0, cols], pj[0:C, 30, :]
            elif m < 12:
                a, b = lora[C:P, 0, cols], pj[C:P, 30, :]
            else:
                a, b = lora[:, 1, cols], pj[:, 31, :]
            nc.tensor.matmul(ps[:, m % 8, 0:N], a, b, start=True, stop=True).then_inc(S("gates_made"), 1)
        pe.wait_ge(S("gates_out"), 18)
        for n, src in ((1, t2), (2, t2)):
            pe.wait_ge(S("head_terms"), n)
            if n == 2:
                pe.wait_ge(S("kk_root"), 1)
            for j in range(RT):
                last = nc.tensor.matmul(ps[:, j, 0:N], blk, src[:, j, :], start=True, stop=True)
            last.then_inc(S("head_sums"), 1)
        pe.wait_ge(S("sample_vectors"), 6)
        for q in range(3):
            last = nc.tensor.transpose(ps[0:96, 6, q * P:q * P + P],
                                       svec[:, 2 * q:2 * q + 2, :].rearrange("p a m -> p (a m)"), ident)
        last.then_inc(S("vectors_turned"), 1)
        pe.wait_ge(S("sample_y"), 2)
        pe.wait_ge(S("gather_in"), 16)
        nc.tensor.matmul(ps[:, 7, 0:48], ycat[:].rearrange("p a e -> p (a e)"), cgat[:, 0:48],
                         start=True, stop=True).then_inc(S("sample_turned_y"), 1)

    def act_gates(act):
        act.wait_ge(S("mixed"), 2)
        nc.scalar.activation(pj[0:C, 30, :], pj[0:C, 30, :], ACT.Tanh).then_inc(S("lora_bent"), 1)
        nc.scalar.activation(pj[:, 31, :], pj[:, 31, :], ACT.Sigmoid).then_inc(S("lora_bent"), 1)
        act.wait_ge(S("mixed"), 20)
        for m in range(18):
            j = m % 6
            act.wait_ge(S("gates_made"), m + 1)
            src = ps[:, m % 8, 0:N]
            if m < 6:
                ins = nc.scalar.activation(sw[:, j, :], src, ACT.Sigmoid, bias=vec("w0", j))
            elif m < 12:
                ins = nc.scalar.activation(aa[:, j, :], src, ACT.Sigmoid, bias=vec("a0", j))
            else:
                ins = nc.scalar.activation(gg[:, j, :], src, ACT.Copy)
            ins.then_inc(S("gates_out"), 1)
        act.wait_ge(S("kk_raw"), 6)
        nc.scalar.activation(t2[:], t1[:], ACT.Square).then_inc(S("head_terms"), 1)
        act.wait_ge(S("head_sums"), 1)
        nc.scalar.activation(t2[:], ps[:, 0:RT, 0:N], ACT.Sqrt).then_inc(S("kk_root"), 1)
        act.wait_ge(S("decay_logs"), 7)
        act.wait_ge(S("kk_made"), 1)
        ex = nc.scalar.activation
        ex(aT[:, :, 0:T], aT[:, :, 0:T], ACT.Exp, scale=-DECAY).then_inc(S("decays"), 1)
        ex(t1[:, :, 0:T], lc[:, :, 0:T], ACT.Exp, scale=DECAY).then_inc(S("decays"), 1)
        ex(svec[:, 1, :].rearrange("p (b j) -> p j b", b=NB), sw[:, :, T:N], ACT.Exp, scale=-DECAY
           ).then_inc(S("sample_vectors"), 1)
        act.wait_ge(S("decays"), 2)
        ex(lc[:, :, 0:T], lc[:, :, 0:T], ACT.Exp, scale=-DECAY).then_inc(S("decays"), 1)
        act.wait_ge(S("vectors_turned"), 1)
        act.wait_ge(S("decayed"), 4)
        nc.scalar.activation(sT[:].rearrange("p q c -> p (q c)"), ps[0:96, 6, 0:384], ACT.Copy
                             ).then_inc(S("vectors_staged"), 1)

    def dve_gates(dve):
        v = nc.vector
        dve.wait_ge(S("sample_split"), 1)
        linked([
            v.tensor_tensor(dif[:, :, 1:T], px[:, :, 0:T - 1], px[:, :, 1:T], ALU.subtract),
            v.tensor_scalar(dif[:, :, 0:1], px[:, :, 0:1], -1.0, None, ALU.mult),
            v.tensor_tensor(dif[:, :, T:N], shT[:], px[:, :, T:N], ALU.subtract),
        ], dve)
        for j in [18, 19] + list(range(18)):
            v.scalar_tensor_tensor(px[:, j, :], dif[:, j, :], vcol[:, 0, VA["mu"] + j:VA["mu"] + j + 1],
                                   px[:, j, :], ALU.mult, ALU.add).then_inc(S("mixed"), 1)
        linked([v.memset(rst[:], 1.0)], dve)
        linked([v.memset(rst[:, 0:T:C], 0.0)], dve)
        dve.wait_ge(S("mixed"), 20)
        for j in range(RT):
            v.tensor_scalar(t1[:, j, :], pkr[:, j, :], vec("kk", j), None, ALU.mult).then_inc(S("kk_raw"), 1)
        dve.wait_ge(S("gates_out"), 6)
        for j in range(RT):
            v.tensor_tensor_scan(lc[:, j, 0:T], rst[:], sw[:, j, 0:T], 0.0, ALU.mult, ALU.add
                                 ).then_inc(S("decay_logs"), 1)
        dve.wait_ge(S("decay_logs"), 6)
        v.tensor_tensor(aT[:, :, 0:T], lc[:, :, 0:T], sw[:, :, 0:T], ALU.subtract).then_inc(S("decay_logs"), 1)
        dve.wait_ge(S("kk_root"), 1)
        link(v.tensor_scalar(t2[:], t2[:], 1e-12, None, ALU.max), dve)
        link(v.reciprocal(t2[:], t2[:]), dve)
        v.tensor_tensor(kk[:], t1[:], t2[:], ALU.mult).then_inc(S("kk_made"), 1)
        dve.wait_ge(S("kk_made"), 1)
        dve.wait_ge(S("gates_out"), 12)
        instrs = [v.tensor_tensor(bT[:], kk[:], aa[:], ALU.mult)]
        for j in range(RT):
            instrs.append(v.tensor_scalar(t2[:, j, :], aa[:, j, :], 1.0, vec("ka", j), ALU.subtract, ALU.mult))
        linked(instrs, dve)
        link(v.scalar_tensor_tensor(pkr, t2[:], 1.0, pkr, ALU.add, ALU.mult), dve)
        linked([v.scalar_tensor_tensor(t2[:, j, :], pr[:, j, :], vec("rk", j), pkr[:, j, :], ALU.mult, ALU.mult)
                for j in range(5)], dve)
        v.scalar_tensor_tensor(t2[:, 5, :], pr[:, 5, :], vec("rk", 5), pkr[:, 5, :], ALU.mult, ALU.mult
                               ).then_inc(S("head_terms"), 1)

        def smp(q):
            return svec[:, q, :].rearrange("p (b j) -> p j b", b=NB)
        v.tensor_scalar(smp(0), kk[:, :, T:N], -1.0, None, ALU.mult).then_inc(S("sample_vectors"), 1)
        for q, src in ((2, bT[:, :, T:N]), (3, pkr[:, :, T:N]), (4, pr[:, :, T:N]), (5, pvr[:, :, T:N])):
            v.tensor_copy(smp(q), src).then_inc(S("sample_vectors"), 1)
        dve.wait_ge(S("head_sums"), 2)
        link(v.tensor_tensor(bv[:], ps[:, 0:RT, 0:N], pvr, ALU.mult), dve)
        dve.wait_ge(S("decays"), 3)
        v.scalar_tensor_tensor(aT[:, :, 0:T], kk[:, :, 0:T], -1.0, aT[:, :, 0:T], ALU.mult, ALU.mult
                               ).then_inc(S("decayed"), 1)
        v.tensor_tensor(bT[:, :, 0:T], bT[:, :, 0:T], t1[:, :, 0:T], ALU.mult).then_inc(S("decayed"), 1)
        v.tensor_tensor(pkr[:, :, 0:T], pkr[:, :, 0:T], t1[:, :, 0:T], ALU.mult).then_inc(S("decayed"), 1)
        link(v.tensor_copy(wc[:], lc[:, :, C - 1:T:C]), dve)
        v.tensor_tensor(pr[:, :, 0:T], pr[:, :, 0:T], lc[:, :, 0:T], ALU.mult).then_inc(S("decayed"), 1)

        dve.wait_ge(S("state_in"), 16)
        dve.wait_ge(S("vectors_back"), 16)
        dve.wait_ge(S("gather_in"), 16)

        def key(q):
            return sv[:, q, :].unsqueeze(1).broadcast_to([96, C, C])

        def val(ap):
            return ap.unsqueeze(2).broadcast_to([96, C, C])
        link(v.tensor_tensor(S2[:], S1[:], key(0), ALU.mult), dve)
        linked([v.tensor_reduce(smal[:, 0:C], S2[:], AX.X, ALU.add),
                v.tensor_tensor(S1[:], S1[:], key(1), ALU.mult)], dve)
        link(v.tensor_tensor(S2[:], val(smal[:, 0:C]), key(2), ALU.mult), dve)
        link(v.tensor_tensor(S1[:], S1[:], S2[:], ALU.add), dve)
        link(v.tensor_tensor(S2[:], val(sv[:, 5, :]), key(3), ALU.mult), dve)
        v.tensor_tensor(S1[:], S1[:], S2[:], ALU.add).then_inc(S("sample_state"), 1)
        dve.wait_ge(S("sample_state"), 1)
        link(v.tensor_tensor(S2[:], S1[:], key(4), ALU.mult), dve)
        link(v.tensor_reduce(smal[:, 0:C], S2[:], AX.X, ALU.add), dve)
        for a in range(2):
            v.tensor_scalar(ycat[:, a, :], smal[:, 0:C], cgat[:, 48 + a:49 + a], None, ALU.mult
                            ).then_inc(S("sample_y"), 1)
        dve.wait_ge(S("sample_turned_y"), 1)
        v.tensor_copy(pvr[:, :, T:N].rearrange("p j b -> p b j"),
                      ps[:, 7, 0:48].rearrange("p (b j) -> p b j", b=NB)).then_inc(S("sample_y_placed"), 1)

    SU, IU, SL = 1, 2, 3
    LEVELS = (2, 4, 8, 16, 32)


    def mask(m, bits=False):
        a = cm[:, m:m + 1, :].unsqueeze(1)
        return (a.bitcast(U32) if bits else a).broadcast_to([P, 2, RT, C])

    def region(r):
        return ps[:, 2 * r:2 * r + 2, 0:RT * C].rearrange("p b (h c) -> p b h c", c=C)

    def spot(r, h):
        return ps[:, 2 * r + h % 2, h // 2 * C:h // 2 * C + C]

    def pos(h):
        return h % 2 * RT + h // 2

    def split(m):
        return m.rearrange("p (b h) c -> p b h c", b=2)

    def feat(h):
        return slice(h % 2 * C, h % 2 * C + C)

    def pe_chunks(pe):
        pe.wait_ge(S("decayed"), 4)
        pe.wait_ge(S("sample_y_placed"), 1)
        for blk2 in range(2):
            cols = slice(blk2 * P, blk2 * P + P)
            if blk2:
                pe.wait_ge(S("chunk_y"), 3)
                pe.wait_ge(S("chunk_state"), 2)
            for x, src in enumerate((pvr, bT, pkr)):
                for j in range(RT):
                    last = nc.tensor.transpose(ps[:, 2 * x + j // 3, j % 3 * P:j % 3 * P + P], src[:, j, cols], ident)
            last.then_inc(S("tokens_turned"), 1)
            pe.wait_ge(S("tokens_staged"), 3 * blk2 + 3)

            def grams(r, left, right):
                for h in range(H):
                    for cp in range(2):
                        c = slice(blk2 * P + cp * C, blk2 * P + cp * C + C)
                        last = nc.tensor.matmul(spot(r, h)[cp * C:cp * C + C, :],
                                                left[feat(h), h // 2, c], right[feat(h), h // 2, c],
                                                start=True, stop=True)
                last.then_inc(S("grams_made"), 1)
            grams(0, bT, aT)
            grams(1, aT, bT)
            grams(2, pkr, aT)
            grams(3, bT, pr)
            pe.wait_ge(S("grams_out"), 6 * blk2 + 1)
            grams(0, pkr, pr)
            pe.wait_ge(S("grams_out"), 6 * blk2 + 6)
            pe.wait_ge(S("x_blocks"), 10 * blk2 + 2)
            for n, lv in enumerate(LEVELS):
                for h in range(H):
                    last = nc.tensor.matmul(spot(0, h), Abd[:, pos(h), :], Zc[:, pos(h), :], start=True, stop=True)
                last.then_inc(S("level_q"), 1)
                pe.wait_ge(S("level_q_out"), 5 * blk2 + n + 1)
                for h in range(H):
                    last = nc.tensor.matmul(spot(1, h), Xbd[:, pos(h), :], Qc[:, pos(h), :], start=True, stop=True)
                last.then_inc(S("level_z"), 1)
                if n < 4:
                    pe.wait_ge(S("level_qbd_out"), 2 * (4 * blk2 + n + 1))
                    for h in range(H):
                        last = nc.tensor.matmul(spot(2, h), Qbd[:, pos(h), :], Xc[:, pos(h), :], start=True, stop=True)
                    last.then_inc(S("level_x"), 1)
                    pe.wait_ge(S("x_blocks"), 2 * (5 * blk2 + n + 2))
                pe.wait_ge(S("z_level"), 5 * blk2 + n + 1)
            for h in range(H):
                for cp in range(2):
                    R = slice(cp * C, cp * C + C)
                    last = nc.tensor.matmul(spot(3 if cp else 0, h)[R, :], Aak[R, pos(h), :],
                                            tok[R, 0, h * C:h * C + C], start=True, stop=True)
            last.then_inc(S("chunk_av"), 1)
            for cp in range(2):
                n = 2 * blk2 + cp
                R = slice(cp * C, cp * C + C)
                c = slice(n * C, n * C + C)
                if n:
                    pe.wait_ge(S("chunk_state"), n)
                    pe.wait_ge(S("chunk_av_out"), 2 * blk2 + 2)
                    for h in range(H):
                        last = nc.tensor.matmul(spot(0, h)[R, :], aT[feat(h), h // 2, c], ST[feat(h), h // 2, :],
                                                start=True, stop=True)
                    last.then_inc(S("chunk_as"), 1)
                    pe.wait_ge(S("chunk_f_out"), n)
                else:
                    pe.wait_ge(S("chunk_av_out"), 1)
                for h in range(H):
                    last = nc.tensor.matmul(spot(1, h)[R, :], Zc[R, pos(h), :], Fc[R, pos(h), :], start=True, stop=True)
                last.then_inc(S("chunk_u"), 1)
                if n:
                    pe.wait_ge(S("chunk_y"), 2 * n - 1)
                    for h in range(H):
                        last = nc.tensor.matmul(ps[feat(h), 6, h // 2 * C:h // 2 * C + C], ST[feat(h), h // 2, :],
                                                pr[feat(h), h // 2, c], start=True, stop=True)
                    last.then_inc(S("chunk_rs"), 1)
                pe.wait_ge(S("chunk_u_out"), n + 1)
                for h in range(H):
                    d = slice(h * C, h * C + C)
                    out = ps[feat(h), 5, h // 2 * C:h // 2 * C + C]
                    nc.tensor.matmul(out, tok[R, 1, d], Uc[R, pos(h), :], start=True, stop=False)
                    last = nc.tensor.matmul(out, tok[R, 2, d], tok[R, 0, d], start=False, stop=True)
                last.then_inc(S("chunk_s"), 1)
                for h in range(H):
                    d = slice(h * C, h * C + C)
                    out = ps[feat(h), 4, h // 2 * C:h // 2 * C + C]
                    nc.tensor.matmul(out, Uc[R, pos(h), :], Arb[R, pos(h), :], start=True, stop=False)
                    last = nc.tensor.matmul(out, tok[R, 0, d], Ark[R, pos(h), :], start=False, stop=True)
                last.then_inc(S("chunk_o"), 1)
        pe.wait_ge(S("chunk_state"), 4)
        pe.wait_ge(S("chunk_y"), 7)
        for j in range(RT):
            last = nc.tensor.transpose(pf[0:C, 3072 + j * P:3072 + j * P + P], ST[:, j, :], ident)
        last.then_inc(S("state_turned"), 1)
        for j in range(RT):
            last = nc.tensor.matmul(ps[:, j, 0:N], blk, pvr[:, j, :], start=True, stop=True)
        last.then_inc(S("group_sums"), 1)
        pe.wait_ge(S("group_squares"), 1)
        for j in range(RT):
            last = nc.tensor.matmul(ps[:, j, 0:N], blk, bT[:, j, :], start=True, stop=True)
        last.then_inc(S("group_sums"), 1)
        pe.wait_ge(S("mixed_all"), 1)

    def act_chunks(act):
        cp = nc.scalar.activation
        for blk2 in range(2):
            act.wait_ge(S("tokens_turned"), blk2 + 1)
            for x in range(3):
                cp(tok[:, x, :].rearrange("p (b c) -> p b c", b=2), ps[:, 2 * x:2 * x + 2, 0:384], ACT.Copy
                   ).then_inc(S("tokens_staged"), 1)
            act.wait_ge(S("x_level"), 5 * blk2 + 1)
            for a in range(2):
                r = slice(a * C, a * C + C)
                cp(Xbd[r, :, r], Xc[r, :, :], ACT.Copy).then_inc(S("x_blocks"), 1)
            for n in range(4):
                act.wait_ge(S("level_q_out"), 5 * blk2 + n + 1)
                for a in range(2):
                    r = slice(a * C, a * C + C)
                    cp(Qbd[r, :, r], Qc[r, :, :], ACT.Copy).then_inc(S("level_qbd_out"), 1)
                act.wait_ge(S("x_level"), 5 * blk2 + n + 2)
                for a in range(2):
                    r = slice(a * C, a * C + C)
                    cp(Xbd[r, :, r], Xc[r, :, :], ACT.Copy).then_inc(S("x_blocks"), 1)
        act.wait_ge(S("state_turned"), 1)
        cp(wkT[:].rearrange("p j c -> p (j c)"), pf[0:C, 3072:3072 + RW], ACT.Copy).then_inc(S("final_state"), 1)
        act.wait_ge(S("group_centred"), 1)
        cp(bT[:], pvr, ACT.Square).then_inc(S("group_squares"), 1)
        act.wait_ge(S("group_sums"), 2)
        cp(bT[:], ps[:, 0:RT, 0:N], ACT.Sqrt, bias=gep, scale=1.0 / C).then_inc(S("group_root"), 1)
        act.wait_ge(S("rwkv_made"), 1)
        cp(mixH[:, 4:10, :], pvr, ACT.Copy).then_inc(S("rwkv_head"), 1)

    def dve_chunks(dve):
        v = nc.vector
        dve.wait_ge(S("masks_in"), 16)
        for blk2 in range(2):
            g = 5 * blk2
            i64 = cm[:, 0, :].unsqueeze(1).broadcast_to([P, H, C])
            if blk2 == 0:
                dve.wait_ge(S("blocks_cleared"), 3)
            linked([v.tensor_copy(Zc[:], i64), v.tensor_copy(Xc[:], i64)], dve)
            dve.wait_ge(S("grams_made"), g + 1)
            v.copy_predicated(split(Zc[:]), mask(4, True), region(0)).then_inc(S("grams_out"), 1)
            dve.wait_ge(S("grams_made"), g + 2)
            v.copy_predicated(split(Xc[:]), mask(5, True), region(1)).then_inc(S("x_level"), 1)
            for a in range(2):
                r = slice(a * C, a * C + C)
                v.tensor_tensor(split(Abd[r, :, r]), region(1)[r], mask(SL)[r], ALU.mult).then_inc(S("grams_out"), 1)
            for x, (m, out) in enumerate(((SU, Aak), (IU, Arb), (IU, Ark))):
                dve.wait_ge(S("grams_made"), g + 3 + x)
                v.tensor_tensor(split(out[:]), region((x + 2) % 4), mask(m), ALU.mult).then_inc(S("grams_out"), 1)
            for n in range(5):
                dve.wait_ge(S("level_q"), g + n + 1)
                v.tensor_copy(split(Qc[:]), region(0)).then_inc(S("level_q_out"), 1)
                dve.wait_ge(S("level_z"), g + n + 1)
                v.copy_predicated(split(Zc[:]), mask(6 + 2 * n, True), region(1)).then_inc(S("z_level"), 1)
                if n < 4:
                    dve.wait_ge(S("level_x"), 4 * blk2 + n + 1)
                    v.copy_predicated(split(Xc[:]), mask(7 + 2 * n, True), region(2)).then_inc(S("x_level"), 1)
            dve.wait_ge(S("chunk_av"), blk2 + 1)
            for cp, r in ((0, 0), (1, 3)):
                R = slice(cp * C, cp * C + C)
                v.tensor_copy(split(Fc[R]), region(r)[R]).then_inc(S("chunk_av_out"), 1)
            for cp in range(2):
                n = 2 * blk2 + cp
                R = slice(cp * C, cp * C + C)
                if n:
                    dve.wait_ge(S("chunk_as"), n)
                    dve.wait_ge(S("chunk_av_out"), 2 * blk2 + 2)
                    v.tensor_tensor(split(Fc[R]), region(0)[R], split(Fc[R]), ALU.add).then_inc(S("chunk_f_out"), 1)
                dve.wait_ge(S("chunk_u"), n + 1)
                v.tensor_copy(split(Uc[R]), region(1)[R]).then_inc(S("chunk_u_out"), 1)
                s5 = ps[:, 5, 0:384].rearrange("p (j c) -> p j c", c=C)
                w = spread(wc[:, :, n], C)
                dve.wait_ge(S("chunk_s"), n + 1)
                if n == 0:
                    v.tensor_tensor(ST[:], s5, w, ALU.mult).then_inc(S("chunk_state"), 1)
                else:
                    dve.wait_ge(S("chunk_rs"), n)
                    link(v.tensor_tensor(ST[:], s5, ST[:], ALU.add), dve)
                    v.tensor_tensor(ST[:], ST[:], w, ALU.mult).then_inc(S("chunk_state"), 1)
                y = pvr[:, :, n * C:n * C + C]
                dve.wait_ge(S("chunk_o"), n + 1)
                v.tensor_copy(y, ps[:, 4, 0:384].rearrange("p (j c) -> p j c", c=C)).then_inc(S("chunk_y"), 1)
                if n:
                    dve.wait_ge(S("chunk_y"), 2 * n)
                    v.tensor_tensor(y, ps[:, 6, 0:384].rearrange("p (j c) -> p j c", c=C), y, ALU.add
                                    ).then_inc(S("chunk_y"), 1)
                dve.wait_ge(S("chunk_state"), n + 1)
        dve.wait_ge(S("chunk_y"), 7)
        dve.wait_ge(S("group_sums"), 1)
        v.scalar_tensor_tensor(pvr, ps[:, 0:RT, 0:N], -1.0 / C, pvr, ALU.mult, ALU.add).then_inc(S("group_centred"), 1)
        dve.wait_ge(S("group_root"), 1)
        link(v.reciprocal(bT[:], bT[:]), dve)
        link(v.tensor_tensor(pvr, pvr, bT[:], ALU.mult), dve)
        linked([v.tensor_scalar(pvr[:, j, :], pvr[:, j, :], vec("lnw", j), vec("lnb", j), ALU.mult, ALU.add)
                for j in range(RT)], dve)
        link(v.tensor_tensor(pvr, pvr, bv[:], ALU.add), dve)
        v.tensor_tensor(pvr, pvr, gg[:], ALU.mult).then_inc(S("rwkv_made"), 1)
        dve.wait_ge(S("rwkv_head"), 1)
        v.tensor_tensor(mixL[:, 4:10, :], pvr, mixH[:, 4:10, :].bitcast(F32), ALU.subtract
                        ).then_inc(S("mixed_all"), 1)

    def act_rwkv(act):
        act_gates(act)
        act_chunks(act)

    def dve_rwkv(dve):
        dve_gates(dve)
        dve_chunks(dve)

    def pe_rwkv(pe):
        pe_gates(pe)
        pe_chunks(pe)

    def pool_last(pool):
        pass

    @block.sync
    def _(sp):
        sp_start(sp)
        sp_ffn(sp, *FFN[0])
        sp_square(sp, "w_in", MT // 2, IN)
        sp_square(sp, "w_out", KT // 2, OUT)
        sp_ffn(sp, *FFN[1])

    @block.scalar
    def _(act):
        act_start(act)
        act_ffn(act, *FFN[0][:3])
        act_in(act)
        for k in range(4):
            head(act, CK, OUT, OUT_PER, 0, k)
        act_shift_conv(act)
        act_attend_prompt(act)
        act_attend_sample(act)
        act_rwkv(act)
        act_out(act)
        act_ffn(act, *FFN[1][:3])

    @block.vector
    def _(dve):
        dve_start(dve)
        dve_ffn(dve, *FFN[0][:3])
        dve_in(dve)
        for k in range(4):
            tail(dve, CK, OUT, OUT_PER, 0, k)
        project(dve, MT // 2 - 1, 0)
        dve_shift_conv(dve)
        dve_attend_prompt(dve)
        dve_attend_sample(dve)
        dve_rwkv(dve)
        dve_out(dve)
        dve_ffn(dve, *FFN[1][:3])

    @block.tensor
    def _(pe):
        pe_start(pe)
        pe_ffn(pe, *FFN[0][:3])
        pe_in(pe)
        pe_shift_conv(pe)
        pe_attend_prompt(pe)
        pe_attend_sample(pe)
        pe_rwkv(pe)
        pe_out(pe)
        pe_ffn(pe, *FFN[1][:3])

    @block.gpsimd
    def _(pool):
        pool_start(pool)
        pool_squares(pool, 0)
        pool_squares(pool, 1)
        pool_shift_conv(pool)
        pool_attend_prompt(pool)
        pool_attend_sample(pool)
        pool_rwkv(pool)
        pool_squares(pool, 2)
        pool_y(pool)
        pool_last(pool)

    ctx.close()


_INS = ['x_prompt', 'x_sample', 'cache_swa_k', 'cache_swa_v', 'state_wkv', 'state_shift', 'state_conv',
        'ffn1_norm', 'ffn1_w_gate', 'ffn1_w_up', 'ffn1_w_down', 'mix_norm', 'w_in', 'q_norm', 'k_norm',
        'rwkv_mu', 'rwkv_w0', 'rwkv_w2', 'rwkv_a0', 'rwkv_a2', 'rwkv_g2', 'rwkv_k_k', 'rwkv_k_a', 'rwkv_r_k',
        'rwkv_ln_w', 'rwkv_ln_b', 'conv_w', 'conv_b', 'w_out',
        'ffn2_norm', 'ffn2_w_gate', 'ffn2_w_up', 'ffn2_w_down']
_OUTS = [((1, 256, 2048), 'float32'), ((8, 1, 2048), 'float32'),
         ((1, 1, 256, 8, 64), 'float32'), ((1, 1, 256, 8, 64), 'float32'),
         ((1, 1, 12, 64, 64), 'float32'), ((1, 1, 2560), 'float32'), ((1, 1, 2, 768), 'float32'),
         ((1, 8, 1, 8, 64), 'float32'), ((1, 8, 1, 8, 64), 'float32'),
         ((1, 8, 12, 64, 64), 'float32'), ((1, 8, 2560), 'float32'), ((1, 8, 2, 768), 'float32')]


def kernel(**inputs):
    import numpy as _np
    import concourse.bacc as _bacc
    from concourse import mybir as _mybir
    from concourse.bass_utils import run_bass_kernel_spmd as _run

    nc = _bacc.Bacc("TRN2", target_bir_lowering=False, num_devices=1)
    arrays, args, outs = {}, {}, []
    for name in _INS:
        arrays[f"in_{name}_dram"] = _np.ascontiguousarray(inputs[name])
    for name, a in tables().items():
        arrays[f"in_{name}_dram"] = _np.ascontiguousarray(a)
    for name, a in arrays.items():
        args[name[3:-5]] = nc.dram_tensor(name, a.shape, _mybir.dt.from_np(a.dtype), kind="ExternalInput").ap()
    for i, (shape, dtype) in enumerate(_OUTS):
        dt = _mybir.dt.from_np(_np.dtype(dtype))
        outs.append(nc.dram_tensor(f"out_{i}_dram", shape, dt, kind="ExternalOutput").ap())
    build(nc, args, outs)
    r = _run(nc, [arrays], core_ids=[0])
    return tuple(r.results[0][f"out_{i}_dram"] for i in range(len(_OUTS)))
```

```python
from contextlib import ExitStack

import numpy as np

import concourse.bass as bass
from concourse import mybir

F32 = mybir.dt.float32
F32R = mybir.dt.float32r
U32 = mybir.dt.uint32
ACT = mybir.ActivationFunctionType
ALU = mybir.AluOpType
AX = mybir.AxisListType

P = 128
D = 2048
FF = 5632
MIX = 6400
T = 256
NB = 8
N = T + NB
KT = D // P
FT = FF // P
MT = MIX // P
CK = 4
CW = 2 * P
RING = 4
RW = 768
RT = RW // P
H = 12
C = 64
PAST = 2048
EPS = 1e-6
GN_EPS = 64e-5
DECAY = float(np.exp(-0.5))
DILATIONS = (1, 4, 16)
SPAN = 128

GU_PER, DN_PER, IN_PER, OUT_PER = 8, 12, 4, 4
GU1 = 0
DN1 = GU1 + GU_PER * FT // 2
IN = DN1 + DN_PER * KT // 2
OUT_K0 = (0, 12, 4, 8)
OUT = IN + IN_PER * MT // 2
GU2 = OUT + OUT_PER * KT // 2
DN2 = GU2 + GU_PER * FT // 2

DN_KT = [4] * 8 + [3] * 4
DN_K0 = [sum(DN_KT[:k]) for k in range(DN_PER)]

VA = dict(ffn1=0, mix=16, ffn2=32, mu=48)
VB = dict(w0=0, a0=6, kk=12, ka=18, rk=24, lnw=30, lnb=36, cw=42, cb=60, qn=66, kn=67)


def slope(h):
    return float(2.0 ** (-8.0 * (h + 1) / 8))


def tables():
    q = np.arange(P)[:, None]
    k = np.arange(P)[None, :]
    own = q - k
    dist = np.concatenate([own, own + P, own], 1)
    mult = ((dist >= 0) & (dist <= SPAN)).astype(np.float32)
    for dil in DILATIONS[1:]:
        mult += (dist >= 0) & (dist % dil == 0)
    dist = np.where(mult > 0, dist, 1e30).astype(np.float32)
    ident = np.eye(P, dtype=np.float32)
    blk = np.kron(np.eye(2), np.ones((C, C))).astype(np.float32)
    i64 = np.concatenate([np.eye(C), np.eye(C)], 0).astype(np.float32)
    r = (np.arange(P) % C)[:, None]
    c = np.arange(C)[None, :]
    m = [i64, (r < c), (r <= c), (r > c)]
    for s in (1, 2, 4, 8, 16, 32):
        up = (r // s % 2 == 0) & (c // s == r // s + 1)
        lo = (c // s % 2 == 0) & (r // s == c // s + 1)
        m += [up, lo]
    masks = np.concatenate([x.astype(np.float32) for x in m], 1)
    alibi = np.zeros((32, 2, 3, P), np.float32)
    for bj in range(32):
        for par in range(2):
            for g, dil in enumerate(DILATIONS):
                alibi[bj, par, g] = -slope(2 * (bj % 4) + par) * dil * (P - np.arange(P))
    rows = np.arange(96)
    gather = (rows[:, None] // 2 == np.arange(48)[None, :]).astype(np.float32)
    parity = (rows[:, None] % 2 == np.arange(2)[None, :]).astype(np.float32)
    heads = np.zeros((P, 22), np.float32)
    heads[0:C, 10] = heads[C:P, 11] = 1
    return {
        "c_base": np.concatenate([ident, blk], 1),
        "c_att": np.concatenate([dist, mult], 1),
        "c_masks": masks,
        "c_alibi": alibi.reshape(32, 768),
        "c_heads": heads, "c_spread": np.kron(np.eye(12), np.ones((1, C))).astype(np.float32),
        "c_gather": np.concatenate([gather, parity], 1),
    }


def build(nc, t, o):
    ctx = ExitStack()
    base = 16512

    def at(name, shape, dt, off):
        return nc.alloc_sbuf_tensor_at(name, shape, dt, offset=base + off)

    raw = at("raw", [P, RING, CK, CW], F32, 0)
    wH = at("wH", [P, RING, CK, CW], F32R, 16384)
    wL = at("wL", [P, RING, CK, CW], F32R, 32768)
    xr = at("xr", [P, KT, N], F32, 49152)
    M0 = 66048
    hH = at("hH", [P, FT, N], F32R, M0)
    hL = at("hL", [P, FT, N], F32R, M0 + 46464)
    xH = at("xH", [P, KT, N], F32R, M0 + 92928)
    xL = at("xL", [P, KT, N], F32R, M0 + 109824)
    E0 = M0 + 126720
    gt = at("gt", [P, 2, N], F32, E0)
    st = at("st", [P, 2, N], F32, E0 + 2112)
    ut = at("ut", [P, 2, N], F32, E0 + 4224)
    hf = at("hf", [P, 2, N], F32, E0 + 6336)
    sq = at("sq", [P, 2, 2, N], F32, E0 + 8448)
    acc = at("acc", [P, 2, N], F32, E0 + 12672)
    K0 = E0 + 14784
    rs = at("rs", [P, N], F32, K0)
    sd = at("sd", [P, N], F32, K0 + 1056)
    vcol = at("vcol", [P, 2, 68], F32, K0 + 2112)
    cb = at("cb", [P, 2 * P], F32, K0 + 2656)
    ones = at("ones", [P, P], F32, K0 + 3680)
    eps = at("eps", [P, 4], F32, K0 + 4192)
    vrowb = at("vrowb", [68, P], F32, K0 + 4224)
    ident, blk = cb[:, 0:P], cb[:, P:2 * P]
    ep, gep = eps[:, 0:1], eps[:, 1:2]

    xin = at("xin", [P, 2, D], F32, M0)
    xsin = at("xsin", [NB, D], F32, M0 + 16384)
    vrowa = at("vrowa", [68, P], F32, M0 + 24576)
    yst = at("yst", [P, 2, 2, CW], F32, M0 + 92928)
    yss = at("yss", [NB, 2, CW], F32, M0 + 92928 + 4096)
    yf = at("yf", [P, 2, 2, N], F32, M0 + 92928 + 6144)

    mixH = at("mixH", [P, KT, N], F32R, M0)
    mixL = at("mixL", [P, KT, N], F32R, M0 + 16896)
    A0 = M0
    PB = M0 + 40128
    pj = at("pj", [P, MT, N], F32, PB)
    crow = at("crow", [96, P], F32, E0 + 1664)
    srow = at("srow", [80, 2, P], F32, E0 + 640)
    zs = at("zs", [P, RT, 3, NB], F32, A0 + 38400)
    zo = at("zo", [P, 10, RT], F32, A0 + 38976)
    zoT = at("zoT", [60, P], F32, E0 + 6144)
    ctmp = at("ctmp", [P, RT, NB], F32, A0 + 39232)
    so = at("so", [P, 2, P], F32, E0 + 6656)
    kv = at("kv", [P, 4, 512], F32, A0)
    catt = at("catt", [P, 768], F32, A0 + 8192)
    sc = at("sc", [P, 8, 384], F32, A0 + 11264)
    rq = at("rq", [P, 8, N], F32, A0 + 23552)
    qkr = at("qkr", [96, P], F32, A0 + 32000)
    kb = [at("kb0", [P, 3, 512], F32, A0 + 23552),
          at("kb1", [P, 3, 512], F32, PB + 30 * N * 4 - 12288),
          at("kb2", [P, 3, 512], F32, PB + 30 * N * 4 - 6144)]
    vb = at("vb", [P, 3, 3, 512], F32, A0 + 11264)
    qb = at("qb", [P, 2, 512], F32, A0 + 32512)
    ss = at("ss", [P, 3, 2, NB, 4], F32, A0 + 36608)
    pS = at("pS", [P, 3, 2, 32], F32, A0 + 37376)
    osm = at("osm", [P, 64], F32, A0 + 38144)
    sa = at("sa", [32, 2, 385], F32, E0 + 8448)
    calb = at("calb", [32, 768], F32, E0 + 11552)
    pex = at("pex", [32, 2, 64], F32, E0 + 5632)
    psf = at("psf", [P, 32], F32, E0 + 5504)
    shc = at("shc", [P, 180], F32, E0 + 4224)
    qkc = at("qkc", [P, 96], F32, E0 + 4960)
    shT = at("shT", [P, 20, NB], F32, E0)
    ST = at("ST", [P, RT, C], F32, E0 + 640)
    wc = at("wc", [P, RT, 4], F32, E0 + 2176)
    am = at("am", [P, 64], F32, E0 + 2272)
    svec = at("svec", [P, 6, 48], F32, E0 + 2528)
    cgat = at("cgat", [96, 50], F32, E0 + 3680)
    smal = at("smal", [96, 66], F32, E0 + 3936)
    G = RT * N * 4
    PR = PB + 12 * N * 4
    aT = at("aT", [P, RT, N], F32, PB)
    bT = at("bT", [P, RT, N], F32, PB + G)
    F0 = PB + 32 * N * 4
    gg = at("gg", [P, RT, N], F32, F0)
    bv = at("bv", [P, RT, N], F32, M0 + 33792)
    L0 = F0 + G
    sw = at("sw", [P, RT, N], F32, L0)
    lc = at("lc", [P, RT, N], F32, L0 + G)
    aa = at("aa", [P, RT, N], F32, L0 + 2 * G)
    kk = at("kk", [P, RT, N], F32, L0 + 3 * G)
    t1 = at("t1", [P, RT, N], F32, L0 + 4 * G)
    t2 = at("t2", [P, RT, N], F32, L0 + 5 * G)
    lora = at("lora", [P, 2, RW], F32, M0 + 4224)
    dif = at("dif", [P, 2, N], F32, E0 + 5344)
    rst = at("rst", [P, T], F32, E0 + 12544)
    hd = at("hd", [P, 22], F32, E0 + 14624)
    hs = at("hs", [H, RW], F32, M0 + 21120)
    hn = at("hn", [H, N], F32, E0 + 13568)
    S1 = at("S1", [96, C, C], F32, 16384)
    S2 = at("S2", [96, C, C], F32, 32768)
    sT = at("sT", [96, 3, P], F32, M0 + 4224)
    sv = at("sv", [96, 6, C], F32, M0 + 5760)
    ycat = at("ycat", [96, 2, C], F32, M0 + 7296)
    cm = at("cm", [P, 16, C], F32, E0 + 8448)
    Abd = at("Abd", [P, H, P], F32, L0)
    Xbd = at("Xbd", [P, H, P], F32, L0 + 6144)
    Qbd = at("Qbd", [P, H, P], F32, L0 + 12288)
    Zc = at("Zc", [P, H, C], F32, L0 + 18432)
    Xc = at("Xc", [P, H, C], F32, L0 + 21504)
    Qc = at("Qc", [P, H, C], F32, L0 + 24576)
    Aak = at("Aak", [P, H, C], F32, L0 + 27648)
    Arb = at("Arb", [P, H, C], F32, L0 + 30720)
    Ark = at("Ark", [P, H, C], F32, L0 + 33792)
    tok = at("tok", [P, 3, RW], F32, L0 + 36864)
    assert L0 + 36864 + 9216 <= E0
    Fc, Uc = Qc, Xc
    wkT = at("wkT", [C, RT, P], F32, L0)
    assert base + K0 + 4736 <= 229344

    ps = ctx.enter_context(nc.psum_tensor("ps", [P, 8, 512], F32))
    sems = {}

    def S(name):
        if name not in sems:
            sems[name] = ctx.enter_context(nc.semaphore(name))
        return sems[name]

    q_dram = nc.dram_tensor("q_rows", (4 * NB, P), F32, kind="Internal").ap()
    s_dram = nc.dram_tensor("wkv_rows", (6 * 48, P), F32, kind="Internal").ap()

    block = ctx.enter_context(nc.Block())

    def w_view(name):
        return t[name][0].rearrange("(kt p) f -> p kt f", p=P)

    views = {n: w_view(n) for n in ("ffn1_w_gate", "ffn1_w_up", "ffn1_w_down", "w_in", "w_out",
                                    "ffn2_w_gate", "ffn2_w_up", "ffn2_w_down")}

    def number(first, per, i, k):
        return i * per + (first + k)

    def load(sp, view, k0, nk, pair, first, per, i, k, fresh=False):
        if not fresh:
            sp.wait_ge(S("tail_made"), number(first, per, i, k) - RING + 1)
        sp.dma_start(raw[:, k % RING, 0:nk, :], view[:, k0:k0 + nk, bass.ds(pair * CW, CW)]
                     ).then_inc(S(f"landed{k % RING}"), 16)

    def head(act, nk, first, per, i, k, fresh=False):
        act.wait_ge(S(f"landed{k % RING}"), i * (16 * (per // RING)) + 16 * (first // RING + k // RING + 1))
        if not fresh:
            act.wait_ge(S("chunk_used"), number(first, per, i, k) - RING + 1)
        nc.scalar.activation(wH[:, k % RING, 0:nk, :], raw[:, k % RING, 0:nk, :], ACT.Copy
                             ).then_inc(S("head_made"), 1)

    def tail(dve, nk, first, per, i, k):
        dve.wait_ge(S("head_made"), number(first, per, i, k) + 1)
        nc.vector.tensor_tensor(wL[:, k % RING, 0:nk, :], raw[:, k % RING, 0:nk, :],
                                wH[:, k % RING, 0:nk, :].bitcast(F32), ALU.subtract
                                ).then_inc(S("tail_made"), 1)

    def products(pe, vH, vL, k0, nk, bank, start, stop, first, per, i, k):
        pe.wait_ge(S("tail_made"), number(first, per, i, k) + 1)
        for q in range(nk):
            for half in range(2):
                cols = slice(half * P, half * P + P)
                out = ps[:, bank + half, 0:N]
                a, b = start and q == 0, stop and q == nk - 1
                nc.tensor.matmul(out, wH[:, k % RING, q, cols], vH[:, k0 + q, :], start=a, stop=False)
                nc.tensor.matmul(out, wH[:, k % RING, q, cols], vL[:, k0 + q, :], start=False, stop=False)
                last = nc.tensor.matmul(out, wL[:, k % RING, q, cols], vH[:, k0 + q, :], start=False, stop=b)
        last.then_inc(S("chunk_used"), 1)

    def two(ap):
        return ap[:].unsqueeze(1).broadcast_to([P, 2, N])


    def early(q):
        return isinstance(q, int) and q < 2

    def squares_and_heads(act, w, q, slot):
        act.wait_ge(S("x_ready"), 8 * w + 1 + q)
        if w or not early(q):
            act.wait_ge(S("squares_added"), 8 * w - 1 + q)
        nc.scalar.activation(sq[:, slot, :, :], xr[:, bass.ds(q * 2, 2), :], ACT.Square
                             ).then_inc(S("squares_made"), 1)
        for e in range(2):
            nc.scalar.activation(xH[:, bass.ds(q * 2 + e, 1), :], xr[:, bass.ds(q * 2 + e, 1), :], ACT.Copy,
                                 scale=vcol[:, 0, bass.ds(q * 2 + (16 * w + e), 1)]
                                 ).then_inc(S("x_head"), 1)

    def x_tails(dve, w, q):
        dve.wait_ge(S("x_head"), 16 * w + 2 + q * 2)
        for e in range(2):
            nc.vector.scalar_tensor_tensor(
                xL[:, bass.ds(q * 2 + e, 1), :], xr[:, bass.ds(q * 2 + e, 1), :],
                vcol[:, 0, bass.ds(q * 2 + (16 * w + e), 1)],
                xH[:, bass.ds(q * 2 + e, 1), :].bitcast(F32), ALU.mult, ALU.subtract
            ).then_inc(S("x_tail"), 1)

    def x_add(dve, w, q, bank, factor, used):
        dve.wait_ge(S("chunk_used"), used)
        nc.vector.scalar_tensor_tensor(xr[:, bass.ds(q * 2, 2), :], ps[:, bank:bank + 2, 0:N], factor,
                                       xr[:, bass.ds(q * 2, 2), :], ALU.mult, ALU.add
                                       ).then_inc(S("x_ready"), 1)

    def norm_sum(pe, w):
        pe.wait_ge(S("squares_added"), 8 * w + 8)
        if w == 0:
            pe.wait_ge(S("constants_set"), 3)
        nc.tensor.matmul(ps[:, 4, 0:N], ones[:], acc[:, 0, :], start=True, stop=False)
        nc.tensor.matmul(ps[:, 4, 0:N], ones[:], acc[:, 1, :], start=False, stop=True
                         ).then_inc(S("norm_summed"), 1)

    def norm_root(act, w):
        act.wait_ge(S("norm_summed"), w + 1)
        nc.scalar.activation(sd[:], ps[:, 4, 0:N], ACT.Sqrt, bias=ep, scale=1.0 / D
                             ).then_inc(S("norm_root"), 1)

    def norm_reciprocal(dve, w):
        dve.wait_ge(S("norm_root"), w + 1)
        nc.vector.reciprocal(rs[:], sd[:]).then_inc(S("norm_ready"), 1)
        dve.wait_ge(S("norm_ready"), w + 1)

    def gate_scale(dve, u, first, p):
        dve.wait_ge(S("chunk_used"), first + 4 + p * GU_PER)
        nc.vector.tensor_tensor(gt[:], ps[:, 0:2, 0:N], two(rs), ALU.mult).then_inc(S("gate_scaled"), 1)

    def gate_silu(act, u, p):
        act.wait_ge(S("gate_scaled"), FT // 2 * u + 1 + p)
        nc.scalar.activation(st[:], gt[:], ACT.Silu).then_inc(S("silu_made"), 1)

    def hidden(dve, u, first, p):
        dve.wait_ge(S("chunk_used"), first + GU_PER + p * GU_PER)
        nc.vector.tensor_tensor(ut[:], ps[:, 2:4, 0:N], two(rs), ALU.mult).then_inc(S("up_scaled"), 1)
        dve.wait_ge(S("up_scaled"), FT // 2 * u + 1 + p)
        dve.wait_ge(S("silu_made"), FT // 2 * u + 1 + p)
        nc.vector.tensor_tensor(hf[:], st[:], ut[:], ALU.mult).then_inc(S("hidden_made"), 1)

    def hidden_head(act, u, p):
        act.wait_ge(S("hidden_made"), FT // 2 * u + 1 + p)
        nc.scalar.activation(hH[:, bass.ds(p * 2, 2), :], hf[:], ACT.Copy).then_inc(S("hidden_head"), 1)

    def hidden_tail(dve, u, p):
        dve.wait_ge(S("hidden_head"), FT // 2 * u + 1 + p)
        nc.vector.tensor_tensor(hL[:, bass.ds(p * 2, 2), :], hf[:], hH[:, bass.ds(p * 2, 2), :].bitcast(F32),
                                ALU.subtract).then_inc(S("hidden_tail"), 1)

    FFN = ((0, GU1, DN1, "ffn1"), (1, GU2, DN2, "ffn2"))

    def sp_ffn(sp, u, gu, dn, name):
        def step(i, fresh=False):
            for k in range(GU_PER):
                load(sp, views[name + ("_w_gate" if k < 4 else "_w_up")], CK * (k % 4), CK, i, gu, GU_PER, i, k,
                     fresh=fresh and k < RING)
        step(0, fresh=u == 0)
        with sp.Fori(1, FT // 2) as i:
            step(i)
        with sp.Fori(0, KT // 2) as i:
            for k in range(DN_PER):
                load(sp, views[name + "_w_down"], DN_K0[k], DN_KT[k], i, dn, DN_PER, i, k)

    def sp_in(sp):
        for lo, hi, shift in ((0, 6, 0), (6, 15, 10), (15, 16, 0), (16, 25, -10)):
            with sp.Fori(lo, hi) as i:
                for k in range(4):
                    load(sp, views["w_in"], CK * k, CK, i + shift, IN, IN_PER, i, k)

    def sp_out(sp):
        with sp.Fori(0, KT // 2) as i:
            for k in range(4):
                load(sp, views["w_out"], OUT_K0[k], CK, i, OUT, OUT_PER, i, k)

    def act_ffn(act, u, gu, dn):
        def gate_up(i, first_pair):
            for k in range(5):
                head(act, CK, gu, GU_PER, i, k, fresh=first_pair and u == 0 and k < RING)
            if not first_pair:
                hidden_head(act, u, i - 1)
            elif u == 1:
                squares_and_heads(act, 2, KT // 2 - 1, 1)
            for k in range(5, GU_PER):
                head(act, CK, gu, GU_PER, i, k)
            if first_pair:
                norm_root(act, 2 * u)
            gate_silu(act, u, i)

        def down(i, jj, first_pair):
            q = i * 2 + jj
            for k in range(5):
                head(act, DN_KT[k], dn + DN_PER * jj, 2 * DN_PER, i, k)
            if first_pair:
                hidden_head(act, u, FT // 2 - 1)
            elif u == 0:
                squares_and_heads(act, 1, q - 1, 1 - jj)
            for k in range(5, 8):
                head(act, DN_KT[k], dn + DN_PER * jj, 2 * DN_PER, i, k)
            if u == 1 and not first_pair:
                stage_y(act, q - 1, 1 - jj)
            for k in range(8, DN_PER):
                head(act, DN_KT[k], dn + DN_PER * jj, 2 * DN_PER, i, k)

        gate_up(0, True)
        with act.Fori(1, FT // 2) as i:
            gate_up(i, False)
        for jj in range(2):
            down(0, jj, jj == 0)
        for jj in range(2 * u):
            down(1, jj, False)
        with act.Fori(1 + u, KT // 4) as i:
            for jj in range(2):
                down(i, jj, False)
        if u == 1:
            stage_y(act, KT // 2 - 1, 1)

    def stage_y(act, q, slot):
        act.wait_ge(S("y_turned"), q + 1)
        if not early(q):
            act.wait_ge(S(f"y_out{slot}"), q * 16 - 16 * slot)
        nc.scalar.activation(yst[:, slot, :, :], ps[:, 2 * slot, :].rearrange("p (b c) -> p b c", b=2), ACT.Copy
                             ).then_inc(S("y_staged"), 1)
        nc.scalar.activation(yss[:, slot, :], ps[0:NB, 2 * slot + 1, 0:CW], ACT.Copy).then_inc(S("y_staged"), 1)

    def act_in(act):
        for k in range(4):
            head(act, CK, IN, IN_PER, 0, k)
        squares_and_heads(act, 1, KT // 2 - 1, 1)
        for k in range(4):
            head(act, CK, IN + 4, IN_PER, 0, k)
        norm_root(act, 1)
        for k in range(4):
            head(act, CK, IN + 8, IN_PER, 0, k)
        beside = {
            7: [lambda: act_squares(act)],
            8: [lambda: act_root(act, 0)],
            9: [lambda: act_root(act, 1)],
            10: [lambda: act_kv(act)],
            14: [lambda: act_exp(act, 0), lambda: act_exp(act, 1)],
            17: [lambda: act_probs(act, 0)],
            18: [lambda: act_probs(act, 1)],
            19: [lambda: act_attended(act)],
            20: [lambda: act_load_values(act, (0, 1, 2))],
            21: [lambda: act_sample_exp(act)],
            23: [lambda: act_load_values(act, (3, 4, 5))],
            24: [lambda: act_load_values(act, (6, 7))],
        }
        for i in range(3, MT // 2):
            for k in range(4):
                head(act, CK, IN, IN_PER, i, k)
            for part in beside.get(i, []):
                part()

    def act_out(act):
        def pair(i, jj):
            for k in range(4):
                head(act, CK, OUT + 4 * jj, 8, i, k)
            squares_and_heads(act, 2, i * 2 + (jj - 1), 1 - jj)
        pair(0, 1)
        with act.Fori(1, KT // 4) as i:
            for jj in range(2):
                pair(i, jj)

    def dve_ffn(dve, u, gu, dn):
        def gate_up(i, first_pair):
            for k in range(4):
                tail(dve, CK, gu, GU_PER, i, k)
            if not first_pair:
                hidden(dve, u, gu, i - 1)
            elif u == 1:
                x_add(dve, 2, KT // 2 - 1, 6, 1.0, GU2)
            tail(dve, CK, gu, GU_PER, i, 4)
            if not first_pair:
                hidden_tail(dve, u, i - 1)
            elif u == 1:
                x_tails(dve, 2, KT // 2 - 1)
            for k in range(5, GU_PER):
                tail(dve, CK, gu, GU_PER, i, k)
            if first_pair:
                norm_reciprocal(dve, 2 * u)
            gate_scale(dve, u, gu, i)

        def down(i, jj, first_pair):
            q = i * 2 + jj
            for k in range(4):
                tail(dve, DN_KT[k], dn + DN_PER * jj, 2 * DN_PER, i, k)
            if first_pair:
                hidden(dve, u, gu, FT // 2 - 1)
            elif u == 0:
                x_add(dve, 1, q - 1, 6 - 2 * jj, 0.5, q * DN_PER + dn)
            else:
                y_add(dve, q - 1, 1 - jj, q * DN_PER + dn)
            tail(dve, DN_KT[4], dn + DN_PER * jj, 2 * DN_PER, i, 4)
            if first_pair:
                hidden_tail(dve, u, FT // 2 - 1)
            elif u == 0:
                x_tails(dve, 1, q - 1)
            for k in range(5, DN_PER):
                tail(dve, DN_KT[k], dn + DN_PER * jj, 2 * DN_PER, i, k)

        gate_up(0, True)
        with dve.Fori(1, FT // 2) as i:
            gate_up(i, False)
        for jj in range(2):
            down(0, jj, jj == 0)
        for jj in range(2 * u):
            down(1, jj, False)
        with dve.Fori(1 + u, KT // 4) as i:
            for jj in range(2):
                down(i, jj, False)
        if u == 1:
            y_add(dve, KT // 2 - 1, 1, dn + DN_PER * KT // 2)

    def y_add(dve, q, slot, used):
        dve.wait_ge(S("chunk_used"), used)
        if not early(q):
            dve.wait_ge(S("y_turned"), q - 1)
        nc.vector.scalar_tensor_tensor(yf[:, slot, :, :], ps[:, 4 + 2 * slot:6 + 2 * slot, 0:N], 0.5,
                                       xr[:, bass.ds(q * 2, 2), :], ALU.mult, ALU.add
                                       ).then_inc(S("x_ready"), 1)

    def column_pair(q):
        return q if q < 6 or q == 15 else q + 10 if q < 15 else q - 10

    def project(dve, q, bank):
        dve.wait_ge(S("chunk_used"), IN + IN_PER + q * IN_PER)
        c = 2 * column_pair(q)
        nc.vector.tensor_tensor(pj[:, c:c + 2, :], ps[:, bank:bank + 2, 0:N], two(rs), ALU.mult
                                ).then_inc(S("projected"), 1)

    def dve_in(dve):
        for k in range(4):
            tail(dve, CK, IN, IN_PER, 0, k)
        x_add(dve, 1, KT // 2 - 1, 6, 0.5, IN)
        x_tails(dve, 1, KT // 2 - 1)
        for k in range(4):
            tail(dve, CK, IN + 4, IN_PER, 0, k)
        norm_reciprocal(dve, 1)
        project(dve, 0, 0)
        for k in range(4):
            tail(dve, CK, IN + 8, IN_PER, 0, k)
        project(dve, 1, 2)
        beside = {
            7: [lambda: dve_vectors(dve)],
            8: [lambda: dve_norm(dve, 0)],
            9: [lambda: dve_norm(dve, 1), lambda: dve_sample_columns(dve)],
            11: [lambda: dve_sample_rows(dve)],
            12: [lambda: dve_scores(dve, 0)],
            13: [lambda: dve_scores(dve, 1), lambda: dve_score_max(dve)],
            14: [lambda: dve_key_scores(dve, (0, 1))],
            15: [lambda: dve_probs(dve, 0), lambda: dve_key_scores(dve, (2,))],
            16: [lambda: dve_probs(dve, 1)],
            17: [lambda: dve_turned_probs(dve, 0), lambda: dve_key_scores(dve, (3, 4))],
            18: [lambda: dve_turned_probs(dve, 1), lambda: dve_key_scores(dve, (5,))],
            19: [lambda: dve_key_scores(dve, (6, 7))],
            20: [lambda: dve_sample_max(dve), lambda: dve_conv_in(dve)],
            21: [lambda: dve_sample_probs(dve), lambda: dve_conv_taps(dve)],
            22: [lambda: dve_turned_sample_probs(dve), lambda: dve_conv_rows(dve), lambda: dve_conv_samples(dve)],
            23: [lambda: dve_token_shift(dve, (15, 16, 17, 18))],
            24: [lambda: dve_token_shift(dve, (19, 20, 21, 22, 23))],
        }
        for i in range(3, MT // 2):
            for k in range(4):
                tail(dve, CK, IN, IN_PER, i, k)
            project(dve, i - 1, 2 * ((i - 1) % 2))
            for part in beside.get(i, []):
                part()

    def dve_out(dve):
        def pair(i, jj):
            for k in range(4):
                tail(dve, CK, OUT + 4 * jj, 8, i, k)
            x_add(dve, 2, i * 2 + (jj - 1), 6 - 2 * jj, 1.0, OUT + 4 * jj + i * 8)
            x_tails(dve, 2, i * 2 + (jj - 1))
        pair(0, 1)
        with dve.Fori(1, KT // 4) as i:
            for jj in range(2):
                pair(i, jj)

    def pe_ffn(pe, u, gu, dn):
        w = 2 * u

        def gate_up(i, first_pair):
            for k in range(GU_PER):
                if first_pair and k < 4:
                    pe.wait_ge(S("x_tail"), 16 * w + 4 * (k + 1))
                if k == 0 and not first_pair:
                    pe.wait_ge(S("gate_scaled"), FT // 2 * u + i)
                if k == 4 and not first_pair:
                    pe.wait_ge(S("up_scaled"), FT // 2 * u + i)
                products(pe, xH, xL, CK * (k % 4), CK, 0 if k < 4 else 2, k % 4 == 0, k % 4 == 3,
                         gu, GU_PER, i, k)
                if k == 3 and first_pair:
                    norm_sum(pe, w)

        def down(i, jj, first_pair):
            q = i * 2 + jj
            if not (isinstance(i, int) and i == 0):
                pe.wait_ge(S("x_ready"), 8 * (w + 1) - 1 + q)
            for k in range(DN_PER):
                if first_pair:
                    pe.wait_ge(S("hidden_tail"), FT // 2 * u + (DN_K0[k] + DN_KT[k] + 1) // 2)
                products(pe, hH, hL, DN_K0[k], DN_KT[k], 4 + 2 * jj, k == 0, k == DN_PER - 1,
                         dn + DN_PER * jj, 2 * DN_PER, i, k)
                if u == 1 and not first_pair and k == 5:
                    turn_y(pe, q - 1, 1 - jj)

        gate_up(0, True)
        with pe.Fori(1, FT // 2) as i:
            gate_up(i, False)
        for jj in range(2):
            down(0, jj, jj == 0)
        for jj in range(2 * u):
            down(1, jj, False)
        with pe.Fori(1 + u, KT // 4) as i:
            for jj in range(2):
                down(i, jj, False)
        if u == 1:
            turn_y(pe, KT // 2 - 1, 1)

    def turn_y(pe, q, slot):
        pe.wait_ge(S("x_ready"), 25 + q)
        if not early(q):
            pe.wait_ge(S("y_staged"), q * 2 - 2)
        for e in range(2):
            for b in range(2):
                nc.tensor.transpose(ps[:, 2 * slot, b * CW + e * P:b * CW + e * P + P],
                                    yf[:, slot, e, b * P:b * P + P], ident)
            last = nc.tensor.transpose(ps[0:NB, 2 * slot + 1, e * P:e * P + P], yf[:, slot, e, T:N], ident)
        last.then_inc(S("y_turned"), 1)

    def pe_in(pe):
        for k in range(4):
            pe.wait_ge(S("x_tail"), 16 + 4 * (k + 1))
            products(pe, xH, xL, CK * k, CK, 0, k == 0, k == 3, IN, IN_PER, 0, k)
        norm_sum(pe, 1)
        for k in range(4):
            products(pe, xH, xL, CK * k, CK, 2, k == 0, k == 3, IN + 4, IN_PER, 0, k)
        for k in range(4):
            if k == 0:
                pe.wait_ge(S("projected"), 1)
            products(pe, xH, xL, CK * k, CK, 0, k == 0, k == 3, IN + 8, IN_PER, 0, k)
        beside = {
            6: [lambda: pe_vectors(pe)],
            7: [lambda: pe_head_sums(pe, 0)],
            8: [lambda: pe_head_sums(pe, 1)],
            9: [lambda: pe_token_major(pe)],
            10: [lambda: pe_sample_rows(pe)],
            11: [lambda: pe_scores(pe, 0)],
            12: [lambda: pe_scores(pe, 1)],
            16: [lambda: pe_turn_probs(pe, 0)],
            17: [lambda: pe_turn_probs(pe, 1)],
            18: [lambda: pe_values(pe)],
            19: [lambda: pe_turn_key_scores(pe)],
            21: [lambda: pe_turn_sample_probs(pe)],
            20: [lambda: pe_turn_state_rows(pe)],
            22: [lambda: pe_sample_values(pe, (0, 1, 2))],
            23: [lambda: pe_sample_values(pe, (3, 4, 5))],
            24: [lambda: pe_sample_values(pe, (6, 7))],
        }
        for i in range(3, MT // 2):
            pe.wait_ge(S("projected"), i - 1)
            for k in range(4):
                products(pe, xH, xL, CK * k, CK, 2 * (i % 2), k == 0, k == 3, IN, IN_PER, i, k)
            for part in beside.get(i, []):
                part()

    def pe_out(pe):
        def pair(i, jj):
            if not (isinstance(i, int) and i == 0):
                pe.wait_ge(S("x_ready"), 15 + jj + i * 2)
            for k in range(4):
                if k == 2 and isinstance(i, int) and i == 0 and jj == 0:
                    pe.wait_ge(S("rwkv_split"), 2)
                products(pe, mixH, mixL, OUT_K0[k], CK, 4 + 2 * jj, k == 0, k == 3, OUT + 4 * jj, 8, i, k)
        for jj in range(2):
            pair(0, jj)
        with pe.Fori(1, KT // 4) as i:
            for jj in range(2):
                pair(i, jj)

    def pool_squares(pool, w):
        def add(q, slot):
            pool.wait_ge(S("squares_made"), 8 * w + 1 + q)
            pool.wait_ge(S("squares_added"), 8 * w + q)
            nc.gpsimd.tensor_tensor(acc[:], acc[:], sq[:, slot, :, :], ALU.add).then_inc(S("squares_added"), 1)
        pool.wait_ge(S("squares_made"), 8 * w + 1)
        nc.gpsimd.tensor_copy(acc[:], sq[:, 0, :, :]).then_inc(S("squares_added"), 1)
        add(1, 1)
        with pool.Fori(1, 4) as i:
            for jj in range(2):
                add(i * 2 + jj, jj)

    def pool_y(pool):
        yp = o[0][0].rearrange("(b p) f -> p b f", p=P)
        ys = o[1].rearrange("b s f -> (b s) f")
        with pool.Fori(0, KT // 4) as i:
            for jj in range(2):
                pool.wait_ge(S("y_staged"), 2 + 2 * jj + i * 4)
                pool.dma_start(yp[:, :, bass.ds(i * (2 * CW) + jj * CW, CW)], yst[:, jj, :, :]
                               ).then_inc(S(f"y_out{jj}"), 16)
                pool.dma_start(ys[:, bass.ds(i * (2 * CW) + jj * CW, CW)], yss[:, jj, :]
                               ).then_inc(S(f"y_out{jj}"), 16)
        for jj in range(2):
            pool.wait_ge(S(f"y_out{jj}"), 32 * (KT // 4))

    def row_view(name, width=None):
        return t[name][0].rearrange("(r c) -> r c", c=P)

    def act_start(act):
        act.dma_start(cb[:], t["c_base"]).then_inc(S("base_in"), 16)
        act.dma_start(xsin[:], t["x_sample"].rearrange("b s f -> (b s) f")).then_inc(S("x_in"), 16)
        for name, r, n in (("ffn1_norm", "ffn1", 16), ("mix_norm", "mix", 16), ("ffn2_norm", "ffn2", 16),
                           ("rwkv_mu", "mu", 20)):
            act.dma_start(vrowa[VA[r]:VA[r] + n, :], row_view(name)).then_inc(S("vectors_a_in"), 16)
        act.wait_ge(S("vectors_a_set"), 1)
        for q in range(KT // 2):
            squares_and_heads(act, 0, q, q % 2)

    def sp_start(sp):
        xp = t["x_prompt"][0].rearrange("(b p) f -> p b f", p=P)
        sp.dma_start(xin[:, :, 0:D // 2], xp[:, :, 0:D // 2]).then_inc(S("x_in"), 16)
        sp.dma_start(xin[:, :, D // 2:D], xp[:, :, D // 2:D]).then_inc(S("x_rest_in"), 16)

    def pool_start(pool):
        nc.gpsimd.memset(ones[:], 1.0).then_inc(S("constants_set"), 1)
        nc.gpsimd.memset(ep, EPS).then_inc(S("constants_set"), 1)
        nc.gpsimd.memset(gep, GN_EPS).then_inc(S("constants_set"), 1)
        for name, r in (("rwkv_w0", "w0"), ("rwkv_a0", "a0"), ("rwkv_k_k", "kk"), ("rwkv_k_a", "ka"),
                        ("rwkv_ln_w", "lnw"), ("rwkv_ln_b", "lnb"), ("conv_b", "cb")):
            pool.dma_start(vrowb[VB[r]:VB[r] + RT, :], row_view(name)).then_inc(S("vectors_b_in"), 16)
        pool.dma_start(vrowb[VB["rk"]:VB["rk"] + RT, :], t["rwkv_r_k"][0].rearrange("(r a) c -> r (a c)", a=2)
                       ).then_inc(S("vectors_b_in"), 16)
        pool.dma_start(vrowb[VB["cw"]:VB["cw"] + 3 * RT, :], t["conv_w"][0].rearrange("i (r c) -> (i r) c", c=P)
                       ).then_inc(S("vectors_b_in"), 16)
        for name, r in (("q_norm", "qn"), ("k_norm", "kn")):
            for a in range(2):
                pool.dma_start(vrowb[VB[r]:VB[r] + 1, a * C:a * C + C], t[name]).then_inc(S("vectors_b_in"), 16)

    def pe_start(pe):
        pe.wait_ge(S("base_in"), 16)
        pe.wait_ge(S("vectors_a_in"), 64)
        nc.tensor.transpose(ps[:, 0, 0:68], vrowa[:], ident[0:68, 0:68]).then_inc(S("vectors_a_turned"), 1)
        pe.wait_ge(S("x_in"), 32)
        for q in range(KT // 2):
            if q >= 2:
                pe.wait_ge(S("x_ready"), q - 1)
            if q == KT // 4:
                pe.wait_ge(S("x_rest_in"), 16)
            for d in (2 * q, 2 * q + 1):
                for b in range(2):
                    nc.tensor.transpose(ps[:, 4 + d % 4, b * P:b * P + P], xin[:, b, d * P:d * P + P], ident)
                last = nc.tensor.transpose(ps[:, 4 + d % 4, T:N], xsin[:, d * P:d * P + P], ident[0:NB, 0:NB])
            last.then_inc(S("x_turned"), 1)

    def dve_start(dve):
        dve.wait_ge(S("vectors_a_turned"), 1)
        nc.vector.tensor_copy(vcol[:, 0, :], ps[:, 0, 0:68]).then_inc(S("vectors_a_set"), 1)
        dve.wait_ge(S("vectors_a_set"), 1)
        for q in range(KT // 2 + 1):
            if q < KT // 2:
                dve.wait_ge(S("x_turned"), q + 1)
                b = 4 + 2 * (q % 2)
                nc.vector.tensor_copy(xr[:, 2 * q:2 * q + 2, :], ps[:, b:b + 2, 0:N]).then_inc(S("x_ready"), 1)
            if q >= 1:
                x_tails(dve, 0, q - 1)

    px = pj[:, 12:32]
    pu, pb, pc = pj[:, 32:38], pj[:, 38:44], pj[:, 44:50]

    def vec(name, j=0, n=1):
        return vcol[:, 1, VB[name] + j:VB[name] + j + n]

    def spread(ap, n):
        return ap.unsqueeze(2).broadcast_to([P, ap.shape[1], n])

    chain = [0]

    def link(ins, dve):
        chain[0] += 1
        ins.then_inc(S("vector_step"), 1)
        dve.wait_ge(S("vector_step"), chain[0])

    def linked(instrs, dve):
        for ins in instrs:
            chain[0] += 1
            ins.then_inc(S("vector_step"), 1)
        dve.wait_ge(S("vector_step"), chain[0])

    def pool_state_rows(pool):
        pool.wait_ge(S("state_rows"), 1)
        pool.dma_start(o[6][0, 0].rearrange("i (r c) -> (i r) c", c=P), zoT[0:12, :]).then_inc(S("written"), 16)
        for b in range(NB):
            pool.dma_start(o[11][0, b, 1, :].rearrange("(r c) -> r c", c=P), zoT[12 + 6 * b:18 + 6 * b, :]
                           ).then_inc(S("written"), 16)
        pool.wait_ge(S("state_rows"), 3)
        pool.dma_start(o[5][0].rearrange("a (r c) -> (a r) c", c=P), so[0:20, 0, :]).then_inc(S("written"), 16)
        shift = o[10][0].rearrange("b (r c) -> (b r) c", c=P)
        pool.dma_start(shift[0:100, :], so[20:120, 0, :]).then_inc(S("written"), 16)
        pool.dma_start(shift[100:160, :], so[0:60, 1, :]).then_inc(S("written"), 16)

    def pe_turn_state_rows(pe):
        pe.wait_ge(S("rows_in"), 32)
        nc.tensor.transpose(ps[:, 7, 192:288], crow[:], ident[0:96, 0:96])
        for h in range(2):
            last = nc.tensor.transpose(ps[:, 7, 288 + 80 * h:368 + 80 * h], srow[:, h, :], ident[0:80, 0:80])
        last.then_inc(S("rows_turned"), 1)

    def pe_shift(pe):
        pe.wait_ge(S("conv_state"), 2)
        pe.wait_ge(S("projected"), MT // 2 - 1)
        nc.tensor.transpose(ps[0:60, 3, 0:P], zo[:].rearrange("p c r -> p (c r)"), ident
                            ).then_inc(S("conv_turned"), 1)
        pe.wait_ge(S("shift_columns"), 10)
        nc.tensor.transpose(ps[0:120, 6, 0:P], shc[:, 0:120], ident)
        nc.tensor.transpose(ps[0:60, 7, 0:P], shc[:, 120:180], ident).then_inc(S("shift_turned"), 1)

    def act_split_conv(act):
        act.wait_ge(S("conv_made"), 1)
        nc.scalar.activation(mixH[:, 10:16, :], pu, ACT.Copy).then_inc(S("conv_head"), 1)

    def act_shift(act):
        act.wait_ge(S("conv_turned"), 1)
        act.wait_ge(S("mixed"), 20)
        nc.scalar.activation(zoT[:], ps[0:60, 3, 0:P], ACT.Copy).then_inc(S("state_rows"), 1)
        act.wait_ge(S("shift_turned"), 1)
        nc.scalar.activation(so[0:120, 0, :], ps[0:120, 6, 0:P], ACT.Copy).then_inc(S("state_rows"), 1)
        nc.scalar.activation(so[0:60, 1, :], ps[0:60, 7, 0:P], ACT.Copy).then_inc(S("state_rows"), 1)

    def dve_conv_rows(dve):
        dve.wait_ge(S("rows_turned"), 1)
        linked([
            nc.vector.tensor_copy(shT[:].rearrange("p r b -> p b r"),
                                  ps[:, 7, 288:448].rearrange("p (b r) -> p b r", r=20)),
            nc.vector.tensor_copy(zs[:, :, 0:2, :].rearrange("p r i b -> p b i r"),
                                  ps[:, 7, 192:288].rearrange("p (b i r) -> p b i r", b=NB, i=2)),
        ], dve)

    def dve_conv_in(dve):
        v = nc.vector
        dve.wait_ge(S("projected"), 15)
        link(v.tensor_tensor(pc, pc, pu, ALU.mult), dve)
        v.tensor_copy(zo[:, 0:2, :].rearrange("p c r -> p r c"), pc[:, :, T - 2:T]).then_inc(S("conv_state"), 1)
        v.tensor_copy(zo[:, 2:10, :].rearrange("p c r -> p r c"), pc[:, :, T:N]).then_inc(S("conv_state"), 1)

    def dve_conv_taps(dve):
        for i in (2, 1, 0):
            back = 2 - i
            for j in range(RT):
                out, src = pu[:, j, back:T], pc[:, j, 0:T - back]
                if i == 2:
                    ins = nc.vector.tensor_scalar(out, src, vec("cw", 12 + j), vec("cb", j), ALU.mult, ALU.add)
                else:
                    ins = nc.vector.scalar_tensor_tensor(out, src, vec("cw", 6 * i + j), out, ALU.mult, ALU.add)
                chain[0] += 1
                ins.then_inc(S("vector_step"), 1)
            dve.wait_ge(S("vector_step"), chain[0])

    def dve_conv_samples(dve):
        v = nc.vector
        smp = pu[:, :, T:N]
        linked([v.tensor_tensor(smp, zs[:, :, 0, :], spread(vec("cw", 0, 6), NB), ALU.mult),
                v.tensor_tensor(ctmp[:], zs[:, :, 1, :], spread(vec("cw", 6, 6), NB), ALU.mult)], dve)
        link(v.tensor_tensor(smp, smp, ctmp[:], ALU.add), dve)
        link(v.tensor_tensor(ctmp[:], pc[:, :, T:N], spread(vec("cw", 12, 6), NB), ALU.mult), dve)
        link(v.tensor_tensor(smp, smp, ctmp[:], ALU.add), dve)
        link(v.tensor_tensor(smp, smp, spread(vec("cb", 0, 6), NB), ALU.add), dve)
        v.tensor_tensor(pu, pu, pb, ALU.mult).then_inc(S("conv_made"), 1)

    def dve_token_shift(dve, steps):
        v = nc.vector
        if steps[0] == 15:
            dve.wait_ge(S("values_used"), 1)
        for q in steps:
            j = 2 * column_pair(q) - 12
            x = px[:, j:j + 2]
            dve.wait_ge(S("projected"), q + 1)
            if q > 15:
                dve.wait_ge(S("mixed"), 2 * (q - 15))
            v.tensor_copy(shc[:].rearrange("p (c r) -> p r c", r=20)[:, j:j + 2, :], x[:, :, T - 1:N]
                          ).then_inc(S("shift_columns"), 1)
            linked([
                v.tensor_tensor(dif[:, :, 1:T], x[:, :, 0:T - 1], x[:, :, 1:T], ALU.subtract),
                v.tensor_scalar(dif[:, :, 0:1], x[:, :, 0:1], -1.0, None, ALU.mult),
                v.tensor_tensor(dif[:, :, T:N], shT[:, j:j + 2, :], x[:, :, T:N], ALU.subtract),
            ], dve)
            dve.wait_ge(S("shift_columns"), q - 14)
            for i in range(2):
                v.scalar_tensor_tensor(x[:, i, :], dif[:, i, :], vcol[:, 0, VA["mu"] + j + i:VA["mu"] + j + i + 1],
                                       x[:, i, :], ALU.mult, ALU.add).then_inc(S("mixed"), 1)

    def dve_split_conv(dve):
        v = nc.vector
        dve.wait_ge(S("sample_kv_out"), 16 * 8)
        dve.wait_ge(S("conv_head"), 1)
        dve.wait_ge(S("conv_made"), 1)
        v.tensor_tensor(mixL[:, 10:16, :], pu, mixH[:, 10:16, :].bitcast(F32), ALU.subtract
                        ).then_inc(S("conv_split"), 1)

    pq, pk, pv = pj[:, 0:4], pj[:, 4:8], pj[:, 8:12]

    def pe_vectors(pe):
        pe.wait_ge(S("vectors_b_in"), 16 * 13)
        nc.tensor.transpose(ps[:, 4, 0:68], vrowb[:], ident[0:68, 0:68]).then_inc(S("vectors_b_turned"), 1)

    def pe_head_sums(pe, g):
        if g == 0:
            pe.wait_ge(S("qk_squared"), 1)
            pe.wait_ge(S("vectors_b_set"), 1)
        else:
            pe.wait_ge(S("qk_root"), 1)
        for j in range(4):
            last = nc.tensor.matmul(ps[:, 4 + j, 0:N], blk, rq[:, 4 * g + j, :], start=True, stop=True)
        last.then_inc(S("qk_summed"), 1)

    def pe_token_major(pe):
        pe.wait_ge(S("qk_root"), 2)
        pe.wait_ge(S("qk_normed"), 2)
        for b in range(2):
            for j in range(4):
                nc.tensor.transpose(ps[:, 4 + b, j * P:j * P + P], pk[:, j, b * P:b * P + P], ident)
                last = nc.tensor.transpose(ps[:, 6 + b, j * P:j * P + P], pv[:, j, b * P:b * P + P], ident)
        last.then_inc(S("kv_turned"), 1)

    def pe_sample_rows(pe):
        pe.wait_ge(S("kv_rows"), 1)
        pe.wait_ge(S("qkv_columns"), 1)
        nc.tensor.transpose(ps[0:96, 4, 0:P], qkc[:], ident).then_inc(S("qkv_turned"), 1)

    def pe_scores(pe, g):
        if g == 0:
            pe.wait_ge(S("sample_rows"), 1)
        for h in range(4 * g, 4 * g + 4):
            f = slice(h % 2 * C, h % 2 * C + C)
            if g:
                pe.wait_ge(S("scores_read"), h - 3)
            nc.tensor.matmul(ps[:, 4 + h % 4, 0:P], pq[f, h // 2, 0:P], pk[f, h // 2, 0:P], start=True, stop=True)
            nc.tensor.matmul(ps[:, 4 + h % 4, P:384], pq[f, h // 2, P:T], pk[f, h // 2, 0:T], start=True, stop=True
                             ).then_inc(S("scores_made"), 1)

    def pe_turn_probs(pe, g):
        pe.wait_ge(S("scores_read"), 8)
        pe.wait_ge(S("probs_made"), 2)
        for h in range(4 * g, 4 * g + 4):
            if g:
                pe.wait_ge(S("probs_a" if h % 2 else "probs_v"), (h - 4) // 2 + 1)
            for b in range(3):
                last = nc.tensor.transpose(ps[:, 4 + h % 4, b * P:b * P + P], sc[:, h, b * P:b * P + P], ident)
            last.then_inc(S("probs_turned"), 1)

    def pe_values(pe):
        pe.wait_ge(S("probs_v"), 4)
        pe.wait_ge(S("probs_a"), 4)
        for h in range(8):
            out = ps[h % 2 * C:h % 2 * C + C, 4 + h // 2, 0:T]
            d = slice(h * C, h * C + C)
            nc.tensor.matmul(out, kv[:, 2, d], sc[:, h, 0:T], start=True, stop=False)
            last = nc.tensor.matmul(out[:, P:T], kv[:, 3, d], sc[:, h, T:384], start=False, stop=True)
        last.then_inc(S("attended"), 1)

    def pe_turn_key_scores(pe):
        pe.wait_ge(S("attend_out"), 1)
        pe.wait_ge(S("key_scores"), NB)
        for a in range(2):
            for g in range(3):
                nc.tensor.transpose(ps[0:32, 4 + a, g * P:g * P + P],
                                    ss[:, g, a, :, :].rearrange("p b j -> p (b j)"), ident)
        pe.wait_ge(S("self_product"), 1)
        nc.tensor.matmul(ps[0:32, 6, 0:2], psf[:], blk[:, 0:P:C], start=True, stop=True
                         ).then_inc(S("keys_turned"), 1)

    def pe_turn_sample_probs(pe):
        pe.wait_ge(S("sample_probs"), 2)
        for g in range(3):
            for a in range(2):
                m = (2 * g + a) * 32
                last = nc.tensor.transpose(ps[:, 7, m:m + 32], sa[:, a, g * P:g * P + P], ident[0:32, 0:32])
        last.then_inc(S("sample_turned"), 1)
        pe.wait_ge(S("self_probs"), 1)
        nc.tensor.matmul(ps[:, 5, 0:32], pex[:].rearrange("p a e -> p (a e)"), ident[0:32, 0:32],
                         start=True, stop=True)

    def pe_sample_values(pe, seqs):
        pe.wait_ge(S("sample_columns"), 1)
        for b in seqs:
            pe.wait_ge(S(f"values_in{b % 3}"), 48 * (b // 3 + 1))
            for j in range(4):
                m = 4 * b + j
                for g in range(3):
                    last = nc.tensor.matmul(ps[:, 4, 2 * m:2 * m + 2], vb[:, b % 3, g, j * P:j * P + P],
                                            pS[:, g, :, m], start=g == 0, stop=g == 2)
            last.then_inc(S("values_used"), 1)

    def act_squares(act):
        act.wait_ge(S("projected"), 6)
        nc.scalar.activation(rq[:], pj[:, 0:8], ACT.Square).then_inc(S("qk_squared"), 1)

    def act_root(act, g):
        act.wait_ge(S("qk_summed"), g + 1)
        nc.scalar.activation(rq[:, 4 * g:4 * g + 4, :], ps[:, 4:8, 0:N], ACT.Sqrt, bias=ep, scale=1.0 / C
                             ).then_inc(S("qk_root"), 1)

    def act_kv(act):
        act.wait_ge(S("kv_turned"), 1)
        nc.scalar.activation(kv[:], ps[:, 4:8, :], ACT.Copy).then_inc(S("kv_rows"), 1)

    def act_exp(act, b):
        if b == 0:
            act.wait_ge(S("score_max"), 1)
        cols = slice(P, 384) if b else slice(0, P)
        for h in range(8):
            nc.scalar.activation(sc[:, h, cols], sc[:, h, cols], ACT.Exp, bias=am[:, 16 + b * 8 + h:17 + b * 8 + h],
                                 scale=0.125).then_inc(S("exp_made"), 1)

    def act_probs(act, g):
        for h in (4 * g + 1, 4 * g + 3):
            act.wait_ge(S("probs_turned"), h + 1)
            nc.scalar.activation(sc[:, h, :], ps[:, 4 + h % 4, 0:384], ACT.Copy).then_inc(S("probs_a"), 1)

    def act_attended(act):
        act.wait_ge(S("attended"), 1)
        nc.scalar.activation(pq[:, :, 0:T], ps[:, 4:8, 0:T], ACT.Copy).then_inc(S("attend_out"), 1)

    def cache_rows(engine, cache, b, dst, signal):
        src = t[cache][0, b].rearrange("s h e -> s (h e)")
        for g, dil in enumerate(DILATIONS):
            if dil == 1:
                keys = src[PAST - P:PAST, :]
            else:
                keys = src[PAST - dil * P:PAST, :].rearrange("(p d) f -> p d f", d=dil)[:, 0, :]
            engine.dma_start(dst[:, g, :], keys).then_inc(S(signal), 16)

    def act_load_values(act, seqs):
        if seqs[0] == 0:
            act.wait_ge(S("attended"), 1)
            act.wait_ge(S("key_scores"), NB)
        for b in seqs:
            if b >= 3:
                act.wait_ge(S("values_used"), b - 2)
            cache_rows(act, "cache_swa_v", b, vb[:, b % 3], f"values_in{b % 3}")

    def act_sample_exp(act):
        act.wait_ge(S("sample_max"), 1)
        for a in range(2):
            nc.scalar.activation(sa[:, a, :], sa[:, a, :], ACT.Exp, bias=smal[0:32, 2 + a:3 + a]
                                 ).then_inc(S("sample_exp"), 1)

    def act_split_attention(act):
        act.wait_ge(S("values_used"), NB)
        act.wait_ge(S("prompt_kv_out"), 32)
        nc.scalar.activation(mixH[:, 0:4, 0:T], pq[:, :, 0:T], ACT.Copy).then_inc(S("attention_head"), 1)
        act.wait_ge(S("sample_out"), 2)
        nc.scalar.activation(mixH[:, 0:4, T:N], osm[:, 32:64].rearrange("p (b j) -> p j b", b=NB), ACT.Copy
                             ).then_inc(S("attention_head"), 1)

    def dve_vectors(dve):
        dve.wait_ge(S("vectors_b_turned"), 1)
        nc.vector.tensor_copy(vcol[:, 1, :], ps[:, 4, 0:68]).then_inc(S("vectors_b_set"), 1)
        dve.wait_ge(S("vectors_b_set"), 1)

    def dve_norm(dve, g):
        v = nc.vector
        r, x = rq[:, 4 * g:4 * g + 4], (pq, pk)[g]
        dve.wait_ge(S("qk_root"), g + 1)
        link(v.reciprocal(r, r), dve)
        v.scalar_tensor_tensor(x, x, vec("kn" if g else "qn"), r, ALU.mult, ALU.mult).then_inc(S("qk_normed"), 1)

    def dve_sample_columns(dve):
        dve.wait_ge(S("qk_normed"), 2)
        nc.vector.tensor_copy(qkc[:].rearrange("p (r b) -> p r b", b=NB), pj[:, 0:12, T:N]
                              ).then_inc(S("qkv_columns"), 1)
        nc.vector.tensor_tensor(psf[:].rearrange("p (b j) -> p j b", b=NB), pq[:, :, T:N], pk[:, :, T:N], ALU.mult
                                ).then_inc(S("self_product"), 1)

    def dve_sample_rows(dve):
        dve.wait_ge(S("qkv_turned"), 1)
        nc.vector.tensor_copy(qkr[:], ps[0:96, 4, 0:P]).then_inc(S("sample_rows"), 1)

    def dve_scores(dve, g):
        if g == 0:
            dve.wait_ge(S("att_tables_in"), 32)
        for h in range(4 * g, 4 * g + 4):
            dve.wait_ge(S("scores_made"), h + 1)
            nc.vector.scalar_tensor_tensor(sc[:, h, :], catt[:, 0:384], -8.0 * slope(h), ps[:, 4 + h % 4, 0:384],
                                           ALU.mult, ALU.add).then_inc(S("scores_read"), 1)

    def dve_score_max(dve):
        v = nc.vector
        dve.wait_ge(S("scores_read"), 8)
        linked([v.tensor_reduce(am[:, 0:8], sc[:, :, 0:P], AX.X, ALU.max),
                v.tensor_reduce(am[:, 8:16], sc[:, :, P:384], AX.X, ALU.max)], dve)
        v.tensor_scalar(am[:, 16:32], am[:, 0:16], -0.125, None, ALU.mult).then_inc(S("score_max"), 1)

    def dve_probs(dve, b):
        v = nc.vector
        w = T if b else P
        cols = slice(P, 384) if b else slice(0, P)
        dve.wait_ge(S("exp_made"), 8 * b + 8)
        mult = catt[:, 384:768][:, cols].unsqueeze(1).broadcast_to([P, 8, w])
        link(v.tensor_tensor(sc[:, :, cols], sc[:, :, cols], mult, ALU.mult), dve)
        link(v.tensor_reduce(am[:, 32 + 8 * b:40 + 8 * b], sc[:, :, cols], AX.X, ALU.add), dve)
        link(v.reciprocal(am[:, 48 + 8 * b:56 + 8 * b], am[:, 32 + 8 * b:40 + 8 * b]), dve)
        v.tensor_tensor(sc[:, :, cols], sc[:, :, cols], spread(am[:, 48 + 8 * b:56 + 8 * b], w), ALU.mult
                        ).then_inc(S("probs_made"), 1)

    def dve_turned_probs(dve, g):
        for h in (4 * g, 4 * g + 2):
            dve.wait_ge(S("probs_turned"), h + 1)
            nc.vector.tensor_copy(sc[:, h, :], ps[:, 4 + h % 4, 0:384]).then_inc(S("probs_v"), 1)

    def dve_key_scores(dve, seqs):
        for b in seqs:
            dve.wait_ge(S("key_products"), b + 1)
            nc.vector.tensor_reduce(ss[:, :, :, b, :].rearrange("p g a j -> p g j a"),
                                    kb[b % 3][:].rearrange("p g (j a e) -> p g j a e", e=C, a=2), AX.X, ALU.add
                                    ).then_inc(S("key_scores"), 1)
        if seqs[-1] == NB - 1:
            dve.wait_ge(S("key_scores"), NB)

    def dve_sample_max(dve):
        v = nc.vector
        dve.wait_ge(S("keys_turned"), 1)
        dve.wait_ge(S("att_tables_in"), 32)
        linked([v.scalar_tensor_tensor(sa[:, :, 0:384], ps[0:32, 4:6, 0:384], 0.125,
                                       calb[:].rearrange("p (a k) -> p a k", a=2), ALU.mult, ALU.add),
                v.tensor_scalar(sa[:, :, 384], ps[0:32, 6, 0:2], 0.125, None, ALU.mult)], dve)
        link(v.tensor_reduce(smal[0:32, 0:2], sa[:], AX.X, ALU.max), dve)
        v.tensor_scalar(smal[0:32, 2:4], smal[0:32, 0:2], -1.0, None, ALU.mult).then_inc(S("sample_max"), 1)

    def dve_sample_probs(dve):
        v = nc.vector
        dve.wait_ge(S("sample_exp"), 2)
        link(v.tensor_scalar(sa[:, :, 384], sa[:, :, 384], 3.0, None, ALU.mult), dve)
        link(v.tensor_reduce(smal[0:32, 4:6], sa[:], AX.X, ALU.add), dve)
        link(v.reciprocal(smal[0:32, 6:8], smal[0:32, 4:6]), dve)
        for a in range(2):
            v.tensor_scalar(sa[:, a, :], sa[:, a, :], smal[0:32, 6 + a:7 + a], None, ALU.mult
                            ).then_inc(S("sample_probs"), 1)
        dve.wait_ge(S("sample_probs"), 2)
        v.tensor_copy(pex[:], sa[:, :, 384:385].broadcast_to([32, 2, C])).then_inc(S("self_probs"), 1)

    def dve_turned_sample_probs(dve):
        dve.wait_ge(S("sample_turned"), 1)
        nc.vector.tensor_copy(pS[:].rearrange("p g a m -> p (g a m)"), ps[:, 7, 0:192]
                              ).then_inc(S("sample_columns"), 1)

    def dve_split_attention(dve):
        v = nc.vector
        dve.wait_ge(S("values_used"), NB)
        osf, oo = osm[:, 0:32], osm[:, 32:64]
        link(v.tensor_tensor(osf.rearrange("p (b j) -> p j b", b=NB),
                             ps[:, 5, 0:32].rearrange("p (b j) -> p j b", b=NB), pv[:, :, T:N], ALU.mult), dve)
        for a in range(2):
            f = slice(a * C, a * C + C)
            v.tensor_tensor(oo[f, :], ps[f, 4, 0:64].rearrange("p (m a) -> p m a", a=2)[:, :, a], osf[f, :], ALU.add
                            ).then_inc(S("sample_out"), 1)
        dve.wait_ge(S("attention_head"), 1)
        v.tensor_tensor(mixL[:, 0:4, 0:T], pq[:, :, 0:T], mixH[:, 0:4, 0:T].bitcast(F32), ALU.subtract
                        ).then_inc(S("attention_split"), 1)
        dve.wait_ge(S("attention_head"), 2)
        dve.wait_ge(S("sample_out"), 2)
        v.tensor_tensor(mixL[:, 0:4, T:N], oo.rearrange("p (b j) -> p j b", b=NB),
                        mixH[:, 0:4, T:N].bitcast(F32), ALU.subtract).then_inc(S("attention_split"), 1)

    def pool_attention(pool):
        pool.dma_start(cgat[:], t["c_gather"]).then_inc(S("rwkv_tables_in"), 16)
        pool.wait_ge(S("projected"), 1)
        pool.wait_ge(S("squares_added"), 16)
        pool.dma_start(catt[:], t["c_att"]).then_inc(S("att_tables_in"), 16)
        pool.dma_start(crow[:], t["state_conv"][0].rearrange("b i (r c) -> (b i r) c", c=P)).then_inc(S("rows_in"), 16)
        pool.dma_start(srow[:], t["state_shift"][0].rearrange("b (r c) -> (b r) c", c=P
                                                              ).rearrange("(h q) c -> q h c", h=2)
                       ).then_inc(S("rows_in"), 16)
        pool.dma_start(o[11][0, :, 0, :], t["state_conv"][0][:, 1, :]).then_inc(S("written"), 16)
        pool.wait_ge(S("norm_summed"), 2)
        pool.dma_start(calb[:], t["c_alibi"]).then_inc(S("att_tables_in"), 16)
        pool.wait_ge(S("sample_rows"), 1)
        pool.dma_start(q_dram, qkr[0:32, :]).then_inc(S("rows_out"), 16)

        def queries(b):
            pool.dma_start(qb[:, b % 2, :].rearrange("p (r c) -> p r c", c=P),
                           q_dram.rearrange("(r b) c -> b r c", b=NB)[b:b + 1].broadcast_to([P, 4, P])
                           ).then_inc(S(f"queries_in{b % 2}"), 16)
        pool.wait_ge(S("qk_normed"), 2)
        for b in range(3):
            cache_rows(pool, "cache_swa_k", b, kb[b], f"keys_in{b}")
        pool.wait_ge(S("rows_out"), 16)
        queries(0)
        queries(1)
        for b in range(NB):
            pool.wait_ge(S(f"keys_in{b % 3}"), 48 * (b // 3 + 1))
            pool.wait_ge(S(f"queries_in{b % 2}"), 16 * (b // 2 + 1))
            q = qb[:, b % 2, :].unsqueeze(1).broadcast_to([P, 3, 512])
            nc.gpsimd.tensor_tensor(kb[b % 3][:], kb[b % 3][:], q, ALU.mult).then_inc(S("key_products"), 1)
            if b + 2 < NB:
                pool.wait_ge(S("key_products"), b + 1)
                queries(b + 2)
            if 1 <= b and b + 2 < NB:
                pool.wait_ge(S("key_scores"), b)
                cache_rows(pool, "cache_swa_k", b + 2, kb[(b + 2) % 3], f"keys_in{(b + 2) % 3}")
        for n, a in ((2, 0), (3, 2)):
            pool.dma_start(o[n][0, 0].rearrange("(b p) h e -> p b (h e)", p=P), kv[:, a:a + 2, :]
                           ).then_inc(S("prompt_kv_out"), 16)
        for n, r in ((7, 32), (8, 64)):
            for j in range(4):
                pool.dma_start(o[n][0, :, 0, 2 * j:2 * j + 2, :].rearrange("b h e -> b (h e)"),
                               qkr[r + 8 * j:r + 8 * j + 8, :]).then_inc(S("sample_kv_out"), 16)
        pool.wait_ge(S("attended"), 1)
        pool.wait_ge(S("sample_kv_out"), 16 * 8)
        pool.wait_ge(S("prompt_kv_out"), 32)
        pool.dma_start(lora[0:C, 0, :], t["rwkv_w2"][0]).then_inc(S("rwkv_tables_in"), 16)
        pool.dma_start(lora[C:P, 0, :], t["rwkv_a2"][0]).then_inc(S("rwkv_tables_in"), 16)
        pool.dma_start(lora[:, 1, :], t["rwkv_g2"][0]).then_inc(S("rwkv_tables_in"), 16)
        pool.wait_ge(S("sample_turned"), 1)
        pool.wait_ge(S("self_probs"), 1)
        pool.dma_start(hd[:], t["c_heads"]).then_inc(S("rwkv_tables_in"), 16)
        pool.dma_start(cm[:], t["c_masks"].rearrange("p (m c) -> p m c", c=C)).then_inc(S("rwkv_tables_in"), 16)
        pool.wait_ge(S("values_used"), NB)
        pool.dma_start(hs[:], t["c_spread"]).then_inc(S("rwkv_tables_in"), 16)
        pool.wait_ge(S("chunk_used"), OUT)
        pool.dma_start(S1[:], t["state_wkv"][0].rearrange("b h v k -> (b h) v k")).then_inc(S("state_in"), 16)

    pr, pkr, pvr = pj[:, 12:18], pj[:, 18:24], pj[:, 24:30]
    pf = ps[:].rearrange("p b c -> p (b c)")

    def pool_rwkv(pool):
        pool.wait_ge(S("vectors_staged"), 1)
        pool.dma_start(s_dram.rearrange("(t p) c -> p t c", p=96), sT[:]).then_inc(S("rows_out"), 16)
        pool.wait_ge(S("rows_out"), 32)
        pool.dma_start(sv[:], s_dram.rearrange("(q m) (a e) -> (m a) q e", q=6, a=2)).then_inc(S("vectors_back"), 16)
        for m in (Abd, Xbd, Qbd):
            if m is Abd:
                pool.wait_ge(S("decayed"), 4)
            nc.gpsimd.memset(m[:], 0.0).then_inc(S("blocks_cleared"), 1)
        pool.wait_ge(S("vectors_back"), 16)
        pool.wait_ge(S("state_in"), 16)
        pool.wait_ge(S("rwkv_tables_in"), 112)

        def key(q):
            return sv[:, q, :].unsqueeze(1).broadcast_to([96, C, C])

        def val(ap):
            return ap.unsqueeze(2).broadcast_to([96, C, C])
        g, steps = nc.gpsimd, [0]

        def step(ins):
            steps[0] += 1
            ins.then_inc(S("pool_step"), 1)
            pool.wait_ge(S("pool_step"), steps[0])

        def key_sum(out):
            w = C // 2
            while w > 1:
                step(g.tensor_tensor(S2[:, :, 0:w], S2[:, :, 0:w], S2[:, :, w:2 * w], ALU.add))
                w //= 2
            step(g.tensor_tensor(out, S2[:, :, 0], S2[:, :, 1], ALU.add))
        step(g.tensor_tensor(S2[:], S1[:], key(0), ALU.mult))
        key_sum(smal[:, 0:C])
        step(g.tensor_tensor(S1[:], S1[:], key(1), ALU.mult))
        step(g.tensor_tensor(S2[:], val(smal[:, 0:C]), key(2), ALU.mult))
        step(g.tensor_tensor(S1[:], S1[:], S2[:], ALU.add))
        step(g.tensor_tensor(S2[:], val(sv[:, 5, :]), key(3), ALU.mult))
        g.tensor_tensor(S1[:], S1[:], S2[:], ALU.add).then_inc(S("sample_state"), 1)
        pool.wait_ge(S("sample_state"), 1)
        pool.dma_start(o[9][0].rearrange("b h v k -> (b h) v k"), S1[:]).then_inc(S("sample_state_out"), 16)
        step(g.tensor_tensor(S2[:], S1[:], key(4), ALU.mult))
        key_sum(smal[:, 0:C])
        for a in range(2):
            g.tensor_scalar(ycat[:, a, :], smal[:, 0:C], cgat[:, 48 + a:49 + a], None, ALU.mult
                            ).then_inc(S("sample_y"), 1)
        pool.wait_ge(S("sample_state_out"), 16)

        def steps_done(instrs):
            for ins in instrs:
                steps[0] += 1
                ins.then_inc(S("pool_step"), 1)
            pool.wait_ge(S("pool_step"), steps[0])
        group_gate(pool, g, 0, steps_done)
        pool.wait_ge(S("final_state"), 1)
        for a in range(2):
            pool.dma_start(o[4][0, 0].rearrange("(j a) v k -> a v j k", a=2)[a], wkT[:, :, a * C:a * C + C]
                           ).then_inc(S("written"), 16)
        pool.wait_ge(S("written"), 16 * (5 + NB + 2))

    def pe_gates(pe):
        pe.wait_ge(S("rwkv_tables_in"), 112)
        pe.wait_ge(S("head_terms"), 1)
        pe.wait_ge(S("projected"), MT // 2)
        for j in range(RT):
            last = nc.tensor.matmul(ps[0:H, 0, 0:N], hd[:, 10 - 2 * j:22 - 2 * j], t2[:, j, :],
                                    start=j == 0, stop=j == RT - 1)
        last.then_inc(S("head_sums"), 1)
        pe.wait_ge(S("state_rows"), 3)
        pe.wait_ge(S("rwkv_tables_in"), 112)
        pe.wait_ge(S("lora_bent"), 2)
        for m in range(18):
            j = m % 6
            if m >= 2:
                pe.wait_ge(S("gates_out"), m - 1)
            if m == 6:
                pe.wait_ge(S("head_scale"), 1)
                pe.wait_ge(S("sample_out"), 2)
                pe.wait_ge(S("state_rows"), 1)
                for i in range(RT):
                    last = nc.tensor.matmul(ps[:, i, 0:N], hs[:, i * P:i * P + P], hn[:], start=True, stop=True)
                last.then_inc(S("head_spread"), 1)
            cols = slice(j * P, j * P + P)
            if m < 6:
                a, b = lora[0:C, 0, cols], pj[0:C, 30, :]
            elif m < 12:
                a, b = lora[C:P, 0, cols], pj[C:P, 30, :]
            else:
                a, b = lora[:, 1, cols], pj[:, 31, :]
            nc.tensor.matmul(ps[:, 6 + m % 2, 0:N], a, b, start=True, stop=True).then_inc(S("gates_made"), 1)
        pe.wait_ge(S("gates_out"), 18)
        pe.wait_ge(S("head_terms"), 2)
        pe.wait_ge(S("kk_made"), 1)
        for j in range(RT):
            last = nc.tensor.matmul(ps[:, j, 0:N], blk, t2[:, j, :], start=True, stop=True)
        last.then_inc(S("head_sums"), 1)
        pe.wait_ge(S("sample_vectors"), 6)
        for q in range(3):
            last = nc.tensor.transpose(ps[0:96, 6, q * P:q * P + P],
                                       svec[:, 2 * q:2 * q + 2, :].rearrange("p a m -> p (a m)"), ident)
        last.then_inc(S("vectors_turned"), 1)

    def act_gates(act):
        act.wait_ge(S("mixed"), 2)
        nc.scalar.activation(pj[0:C, 30, :], pj[0:C, 30, :], ACT.Tanh).then_inc(S("lora_bent"), 1)
        nc.scalar.activation(pj[:, 31, :], pj[:, 31, :], ACT.Sigmoid).then_inc(S("lora_bent"), 1)
        act.wait_ge(S("kk_raw"), 6)
        nc.scalar.activation(t2[:], t1[:], ACT.Square).then_inc(S("head_terms"), 1)
        act_split_attention(act)
        act_split_conv(act)
        act_shift(act)
        act.wait_ge(S("head_sums"), 1)
        nc.scalar.activation(hn[:], ps[0:H, 0, 0:N], ACT.Sqrt).then_inc(S("head_root"), 1)
        act.wait_ge(S("mixed"), 20)
        act.wait_ge(S("conv_split"), 1)
        for m in range(18):
            j = m % 6
            act.wait_ge(S("gates_made"), m + 1)
            src = ps[:, 6 + m % 2, 0:N]
            if m < 6:
                ins = nc.scalar.activation(sw[:, j, :], src, ACT.Sigmoid, bias=vec("w0", j))
            elif m < 12:
                ins = nc.scalar.activation(aa[:, j, :], src, ACT.Sigmoid, bias=vec("a0", j))
            else:
                ins = nc.scalar.activation(gg[:, j, :], src, ACT.Copy)
            ins.then_inc(S("gates_out"), 1)
        act.wait_ge(S("decay_logs"), 7)
        act.wait_ge(S("kk_made"), 1)
        ex = nc.scalar.activation
        ex(aT[:, :, 0:T], aT[:, :, 0:T], ACT.Exp, scale=-DECAY).then_inc(S("decays"), 1)
        ex(t1[:, :, 0:T], lc[:, :, 0:T], ACT.Exp, scale=DECAY).then_inc(S("decays"), 1)
        ex(svec[:, 1, :].rearrange("p (b j) -> p j b", b=NB), sw[:, :, T:N], ACT.Exp, scale=-DECAY
           ).then_inc(S("sample_vectors"), 1)
        act.wait_ge(S("decays"), 2)
        ex(lc[:, :, 0:T], lc[:, :, 0:T], ACT.Exp, scale=-DECAY).then_inc(S("decays"), 1)
        act.wait_ge(S("vectors_turned"), 1)
        nc.scalar.activation(sT[:].rearrange("p q c -> p (q c)"), ps[0:96, 6, 0:384], ACT.Copy
                             ).then_inc(S("vectors_staged"), 1)

    def dve_gates(dve):
        v = nc.vector
        dve_token_shift(dve, (24,))
        dve.wait_ge(S("conv_turned"), 1)
        dve.wait_ge(S("conv_made"), 1)
        for j in range(RT):
            v.tensor_scalar(t1[:, j, :], pkr[:, j, :], vec("kk", j), None, ALU.mult).then_inc(S("kk_raw"), 1)
        linked([v.memset(rst[:], 1.0)], dve)
        linked([v.memset(rst[:, 0:T:C], 0.0)], dve)
        dve.wait_ge(S("mixed"), 20)
        dve_split_attention(dve)
        dve_split_conv(dve)
        dve.wait_ge(S("head_root"), 1)
        link(v.tensor_scalar(hn[:], hn[:], 1e-12, None, ALU.max), dve)
        v.reciprocal(hn[:], hn[:]).then_inc(S("head_scale"), 1)
        dve.wait_ge(S("gates_out"), 6)
        for j in range(RT):
            v.tensor_tensor_scan(lc[:, j, 0:T], rst[:], sw[:, j, 0:T], 0.0, ALU.mult, ALU.add
                                 ).then_inc(S("decay_logs"), 1)
        dve.wait_ge(S("decay_logs"), 6)
        v.tensor_tensor(aT[:, :, 0:T], lc[:, :, 0:T], sw[:, :, 0:T], ALU.subtract).then_inc(S("decay_logs"), 1)
        dve.wait_ge(S("head_spread"), 1)
        v.tensor_tensor(kk[:], t1[:], ps[:, 0:RT, 0:N], ALU.mult).then_inc(S("kk_made"), 1)
        dve.wait_ge(S("kk_made"), 1)
        dve.wait_ge(S("gates_out"), 12)
        instrs = [v.tensor_tensor(bT[:], kk[:], aa[:], ALU.mult)]
        for j in range(RT):
            instrs.append(v.tensor_scalar(t2[:, j, :], aa[:, j, :], 1.0, vec("ka", j), ALU.subtract, ALU.mult))
        linked(instrs, dve)
        link(v.scalar_tensor_tensor(pkr, t2[:], 1.0, pkr, ALU.add, ALU.mult), dve)
        linked([v.scalar_tensor_tensor(t2[:, j, :], pr[:, j, :], vec("rk", j), pkr[:, j, :], ALU.mult, ALU.mult)
                for j in range(5)], dve)
        v.scalar_tensor_tensor(t2[:, 5, :], pr[:, 5, :], vec("rk", 5), pkr[:, 5, :], ALU.mult, ALU.mult
                               ).then_inc(S("head_terms"), 1)

        def smp(q):
            return svec[:, q, :].rearrange("p (b j) -> p j b", b=NB)
        v.tensor_scalar(smp(0), kk[:, :, T:N], -1.0, None, ALU.mult).then_inc(S("sample_vectors"), 1)
        for q, src in ((2, bT[:, :, T:N]), (3, pkr[:, :, T:N]), (4, pr[:, :, T:N]), (5, pvr[:, :, T:N])):
            v.tensor_copy(smp(q), src).then_inc(S("sample_vectors"), 1)
        dve.wait_ge(S("head_sums"), 2)
        link(v.tensor_tensor(bv[:], ps[:, 0:RT, 0:N], pvr, ALU.mult), dve)
        dve.wait_ge(S("decays"), 3)
        v.scalar_tensor_tensor(aT[:, :, 0:T], kk[:, :, 0:T], -1.0, aT[:, :, 0:T], ALU.mult, ALU.mult
                               ).then_inc(S("decayed"), 1)
        v.tensor_tensor(bT[:, :, 0:T], bT[:, :, 0:T], t1[:, :, 0:T], ALU.mult).then_inc(S("decayed"), 1)
        v.tensor_tensor(pkr[:, :, 0:T], pkr[:, :, 0:T], t1[:, :, 0:T], ALU.mult).then_inc(S("decayed"), 1)
        link(v.tensor_copy(wc[:], lc[:, :, C - 1:T:C]), dve)
        v.tensor_tensor(pr[:, :, 0:T], pr[:, :, 0:T], lc[:, :, 0:T], ALU.mult).then_inc(S("decayed"), 1)

    SU, IU, SL = 1, 2, 3
    LEVELS = (2, 4, 8, 16, 32)


    def mask(m, bits=False):
        a = cm[:, m:m + 1, :].unsqueeze(1)
        return (a.bitcast(U32) if bits else a).broadcast_to([P, 2, RT, C])

    def region(r):
        return ps[:, 2 * r:2 * r + 2, 0:RT * C].rearrange("p b (h c) -> p b h c", c=C)

    def spot(r, h):
        return ps[:, 2 * r + h % 2, h // 2 * C:h // 2 * C + C]

    def pos(h):
        return h % 2 * RT + h // 2

    def split(m):
        return m.rearrange("p (b h) c -> p b h c", b=2)

    def feat(h):
        return slice(h % 2 * C, h % 2 * C + C)

    def heads(b):
        return range(b, H, 2)

    def half(m, b):
        return m[:, b * RT:b * RT + RT, :]

    def bank(r, b):
        return ps[:, 2 * r + b, 0:RT * C].rearrange("p (h c) -> p h c", c=C)

    def half_mask(m, bits=False):
        a = cm[:, m:m + 1, :]
        return (a.bitcast(U32) if bits else a).broadcast_to([P, RT, C])

    def pe_chunks(pe):
        pe.wait_ge(S("decayed"), 4)
        pe.wait_ge(S("vectors_staged"), 1)
        for blk2 in range(2):
            cols = slice(blk2 * P, blk2 * P + P)
            if blk2:
                pe.wait_ge(S("chunk_y"), 3)
                pe.wait_ge(S("chunk_state"), 2)
            for x, src in enumerate((pvr, bT, pkr)):
                for j in range(RT):
                    last = nc.tensor.transpose(ps[:, 2 * x + j // 3, j % 3 * P:j % 3 * P + P], src[:, j, cols], ident)
            last.then_inc(S("tokens_turned"), 1)
            pe.wait_ge(S("tokens_staged"), 3 * blk2 + 3)

            def grams(r, left, right):
                for h in range(H):
                    for cp in range(2):
                        c = slice(blk2 * P + cp * C, blk2 * P + cp * C + C)
                        last = nc.tensor.matmul(spot(r, h)[cp * C:cp * C + C, :],
                                                left[feat(h), h // 2, c], right[feat(h), h // 2, c],
                                                start=True, stop=True)
                last.then_inc(S("grams_made"), 1)
            grams(0, bT, aT)
            grams(1, aT, bT)
            grams(2, pkr, aT)
            grams(3, bT, pr)
            pe.wait_ge(S("grams_out"), 6 * blk2 + 1)
            grams(0, pkr, pr)
            pe.wait_ge(S("grams_out"), 6 * blk2 + 6)
            if blk2:
                pe_group_sums(pe, 0)
            for n, lv in enumerate(LEVELS):
                m = 10 * blk2 + 2 * n
                for b in range(2):
                    if n:
                        pe.wait_ge(S("z_level"), m - 1 + b)
                    for h in heads(b):
                        last = nc.tensor.matmul(spot(0, h), Abd[:, pos(h), :], Zc[:, pos(h), :], start=True, stop=True)
                    last.then_inc(S("level_q"), 1)
                for b in range(2):
                    pe.wait_ge(S("level_q_out"), m + b + 1)
                    pe.wait_ge(S("x_blocks"), 2 * (m + b + 1))
                    for h in heads(b):
                        last = nc.tensor.matmul(spot(1, h), Xbd[:, pos(h), :], Qc[:, pos(h), :], start=True, stop=True)
                    last.then_inc(S("level_z"), 1)
                if n < 4:
                    for b in range(2):
                        pe.wait_ge(S("level_qbd_out"), 2 * (8 * blk2 + 2 * n + b + 1))
                        for h in heads(b):
                            last = nc.tensor.matmul(spot(2, h), Qbd[:, pos(h), :], Xc[:, pos(h), :],
                                                    start=True, stop=True)
                        last.then_inc(S("level_x"), 1)
                if blk2 and n == 1:
                    pe_group_squares(pe, 0)
                if blk2 and n == 3:
                    pe_group_spread(pe, 0)
            for b in range(2):
                pe.wait_ge(S("z_level"), 10 * blk2 + 9 + b)
                if blk2:
                    pe.wait_ge(S("group_scaled"), 1)
                for h in heads(b):
                    for cp in range(2):
                        R = slice(cp * C, cp * C + C)
                        last = nc.tensor.matmul(spot(3 if cp else 0, h)[R, :], Aak[R, pos(h), :],
                                                tok[R, 0, h * C:h * C + C], start=True, stop=True)
                last.then_inc(S("chunk_av"), 1)
            for cp in range(2):
                n = 2 * blk2 + cp
                R = slice(cp * C, cp * C + C)
                c = slice(n * C, n * C + C)
                if n:
                    pe.wait_ge(S("chunk_state"), n)
                    for b in range(2):
                        pe.wait_ge(S("chunk_av_out"), 4 * blk2 + 2 * b + 2)
                        for h in heads(b):
                            last = nc.tensor.matmul(spot(0, h)[R, :], aT[feat(h), h // 2, c],
                                                    ST[feat(h), h // 2, :], start=True, stop=True)
                        last.then_inc(S("chunk_as"), 1)
                for b in range(2):
                    if n:
                        pe.wait_ge(S("chunk_f_out"), 2 * n - 1 + b)
                    else:
                        pe.wait_ge(S("chunk_av_out"), 2 * b + 1)
                    for h in heads(b):
                        last = nc.tensor.matmul(spot(1, h)[R, :], Zc[R, pos(h), :], Fc[R, pos(h), :],
                                                start=True, stop=True)
                    last.then_inc(S("chunk_u"), 1)
                if n:
                    pe.wait_ge(S("chunk_y"), 2 * n - 1)
                    for h in range(H):
                        last = nc.tensor.matmul(ps[feat(h), 6, h // 2 * C:h // 2 * C + C], ST[feat(h), h // 2, :],
                                                pr[feat(h), h // 2, c], start=True, stop=True)
                    last.then_inc(S("chunk_rs"), 1)
                if n == 3:
                    pe.wait_ge(S("sample_y"), 2)
                    pe.wait_ge(S("rwkv_tables_in"), 112)
                    pe.wait_ge(S("chunk_av_out"), 8)
                    nc.tensor.matmul(ps[:, 7, 0:48], ycat[:].rearrange("p a e -> p (a e)"), cgat[:, 0:48],
                                     start=True, stop=True).then_inc(S("sample_turned_y"), 1)

                def state_products():
                    pe.wait_ge(S("chunk_u_out"), 2 * n + 2)
                    for h in range(H):
                        d = slice(h * C, h * C + C)
                        out = ps[feat(h), 5, h // 2 * C:h // 2 * C + C]
                        nc.tensor.matmul(out, tok[R, 1, d], Uc[R, pos(h), :], start=True, stop=False)
                        last = nc.tensor.matmul(out, tok[R, 2, d], tok[R, 0, d], start=False, stop=True)
                    last.then_inc(S("chunk_s"), 1)

                def output_products():
                    pe.wait_ge(S("chunk_u_out"), 2 * n + 2)
                    for h in range(H):
                        d = slice(h * C, h * C + C)
                        out = ps[feat(h), 4, h // 2 * C:h // 2 * C + C]
                        nc.tensor.matmul(out, Uc[R, pos(h), :], Arb[R, pos(h), :], start=True, stop=False)
                        last = nc.tensor.matmul(out, tok[R, 0, d], Ark[R, pos(h), :], start=False, stop=True)
                    last.then_inc(S("chunk_o"), 1)
                if n < 3:
                    state_products()
                    output_products()
                else:
                    output_products()
                    state_products()
        pe.wait_ge(S("chunk_y"), 7)
        pe.wait_ge(S("sample_y_placed"), 1)
        pe_group_sums(pe, 1)
        pe.wait_ge(S("chunk_state"), 4)
        for j in range(RT):
            last = nc.tensor.transpose(pf[0:C, 3072 + j * P:3072 + j * P + P], ST[:, j, :], ident)
        last.then_inc(S("state_turned"), 1)
        pe_group_squares(pe, 1)
        pe_group_spread(pe, 1)

    GROUP = ((slice(0, P), 6), (slice(P, N), 0))

    def group_bank(part):
        cols, b = GROUP[part]
        w = cols.stop - cols.start
        return ps[:, b:b + 2, 0:3 * w].rearrange("p b (j c) -> p b j c", c=w)

    def tiles(m, cols):
        return m[:, :, cols].rearrange("p (b j) c -> p b j c", b=2)

    def pe_group_sums(pe, part):
        cols, _ = GROUP[part]
        for j in range(RT):
            last = nc.tensor.matmul(group_bank(part)[:, j // 3, j % 3, :], blk, pvr[:, j, cols], start=True, stop=True)
        last.then_inc(S("group_sums"), 1)

    def pe_group_squares(pe, part):
        cols, b = GROUP[part]
        pe.wait_ge(S("group_squares"), part + 1)
        for j in range(RT):
            last = nc.tensor.matmul(ps[0:H, b, 0:cols.stop - cols.start], hd[:, 10 - 2 * j:22 - 2 * j], bT[:, j, cols],
                                    start=j == 0, stop=j == RT - 1)
        last.then_inc(S("group_squared"), 1)

    def pe_group_spread(pe, part):
        cols, _ = GROUP[part]
        pe.wait_ge(S("head_scale"), part + 2)
        for j in range(RT):
            last = nc.tensor.matmul(group_bank(part)[:, j // 3, j % 3, :], hs[:, j * P:j * P + P], hn[:, cols],
                                    start=True, stop=True)
        last.then_inc(S("head_spread"), 1)

    def dve_group_centre(dve, part):
        cols, _ = GROUP[part]
        dve.wait_ge(S("group_sums"), part + 1)
        nc.vector.scalar_tensor_tensor(tiles(pvr, cols), group_bank(part), -1.0 / C, tiles(pvr, cols),
                                       ALU.mult, ALU.add).then_inc(S("group_centred"), 1)

    def act_group_squares(act, part):
        cols, _ = GROUP[part]
        act.wait_ge(S("group_centred"), part + 1)
        nc.scalar.activation(bT[:, :, cols], pvr[:, :, cols], ACT.Square).then_inc(S("group_squares"), 1)

    def act_group_root(act, part):
        cols, b = GROUP[part]
        act.wait_ge(S("group_squared"), part + 1)
        nc.scalar.activation(hn[:, cols], ps[0:H, b, 0:cols.stop - cols.start], ACT.Sqrt, bias=eps[0:H, 1:2],
                             scale=1.0 / C).then_inc(S("head_root"), 1)

    def dve_group_scale(dve, part):
        cols, _ = GROUP[part]
        dve.wait_ge(S("head_root"), part + 2)
        nc.vector.reciprocal(hn[:, cols], hn[:, cols]).then_inc(S("head_scale"), 1)

    def dve_group_scaled(dve, part):
        cols, _ = GROUP[part]
        dve.wait_ge(S("head_spread"), part + 2)
        nc.vector.tensor_tensor(tiles(pvr, cols), tiles(pvr, cols), group_bank(part), ALU.mult
                                ).then_inc(S("group_scaled"), 1)

    def group_gate(engine, side, part, step):
        cols, _ = GROUP[part]
        y = pvr[:, :, cols]
        engine.wait_ge(S("group_scaled"), part + 1)
        step([side.tensor_scalar(y[:, j, :], y[:, j, :], vec("lnw", j), vec("lnb", j), ALU.mult, ALU.add)
              for j in range(RT)])
        step([side.tensor_tensor(y, y, bv[:, :, cols], ALU.add)])
        side.tensor_tensor(y, y, gg[:, :, cols], ALU.mult).then_inc(S("rwkv_made"), 1)

    def act_rwkv_head(act, part):
        cols, _ = GROUP[part]
        act.wait_ge(S("rwkv_made"), part + 1)
        nc.scalar.activation(mixH[:, 4:10, cols], pvr[:, :, cols], ACT.Copy).then_inc(S("rwkv_head"), 1)

    def dve_rwkv_tail(dve, part):
        cols, _ = GROUP[part]
        dve.wait_ge(S("rwkv_head"), part + 1)
        nc.vector.tensor_tensor(mixL[:, 4:10, cols], pvr[:, :, cols], mixH[:, 4:10, cols].bitcast(F32), ALU.subtract
                                ).then_inc(S("rwkv_split"), 1)

    def act_chunks(act):
        cp = nc.scalar.activation

        def blocks(dst, src, name):
            wait, count = name
            for b in range(2):
                act.wait_ge(S(wait), count + b)
                for a in range(2):
                    r = slice(a * C, a * C + C)
                    cp(half(dst, b)[r, :, r], half(src, b)[r, :, :], ACT.Copy
                       ).then_inc(S("x_blocks" if dst is Xbd else "level_qbd_out"), 1)
        for blk2 in range(2):
            act.wait_ge(S("tokens_turned"), blk2 + 1)
            for x in range(3):
                cp(tok[:, x, :].rearrange("p (b c) -> p b c", b=2), ps[:, 2 * x:2 * x + 2, 0:384], ACT.Copy
                   ).then_inc(S("tokens_staged"), 1)
            blocks(Xbd, Xc, ("x_level", 10 * blk2 + 1))
            for n in range(4):
                blocks(Qbd, Qc, ("level_q_out", 10 * blk2 + 2 * n + 1))
                blocks(Xbd, Xc, ("x_level", 10 * blk2 + 2 * n + 3))
                if blk2 and n == 0:
                    act_group_squares(act, 0)
                    act.wait_ge(S("sample_state_out"), 16)
                    act.wait_ge(S("sample_y"), 2)
                if blk2 and n == 1:
                    act_group_root(act, 0)
                if blk2:
                    head(act, CK, OUT, OUT_PER, 0, n)
        act.wait_ge(S("sample_turned_y"), 1)
        act_rwkv_head(act, 0)
        act_group_squares(act, 1)
        act_group_root(act, 1)
        act.wait_ge(S("state_turned"), 1)
        cp(wkT[:].rearrange("p j c -> p (j c)"), pf[0:C, 3072:3072 + RW], ACT.Copy).then_inc(S("final_state"), 1)
        act_rwkv_head(act, 1)

    def dve_chunks(dve):
        v = nc.vector
        dve.wait_ge(S("rwkv_tables_in"), 112)
        for blk2 in range(2):
            g = 5 * blk2
            i64 = cm[:, 0, :].unsqueeze(1).broadcast_to([P, H, C])
            if blk2 == 0:
                dve.wait_ge(S("blocks_cleared"), 3)
            linked([v.tensor_copy(Zc[:], i64), v.tensor_copy(Xc[:], i64)], dve)
            dve.wait_ge(S("grams_made"), g + 1)
            v.copy_predicated(split(Zc[:]), mask(4, True), region(0)).then_inc(S("grams_out"), 1)
            dve.wait_ge(S("grams_made"), g + 2)
            for b in range(2):
                v.copy_predicated(half(Xc, b), half_mask(5, True), bank(1, b)).then_inc(S("x_level"), 1)
            for a in range(2):
                r = slice(a * C, a * C + C)
                v.tensor_tensor(split(Abd[r, :, r]), region(1)[r], mask(SL)[r], ALU.mult).then_inc(S("grams_out"), 1)
            for x, (m, out) in enumerate(((SU, Aak), (IU, Arb), (IU, Ark))):
                dve.wait_ge(S("grams_made"), g + 3 + x)
                v.tensor_tensor(split(out[:]), region((x + 2) % 4), mask(m), ALU.mult).then_inc(S("grams_out"), 1)
            for n in range(5):
                m = 10 * blk2 + 2 * n
                for b in range(2):
                    dve.wait_ge(S("level_q"), m + b + 1)
                    v.tensor_copy(half(Qc, b), bank(0, b)).then_inc(S("level_q_out"), 1)
                for b in range(2):
                    dve.wait_ge(S("level_z"), m + b + 1)
                    v.copy_predicated(half(Zc, b), half_mask(6 + 2 * n, True), bank(1, b)).then_inc(S("z_level"), 1)
                if n < 4:
                    for b in range(2):
                        dve.wait_ge(S("level_x"), 8 * blk2 + 2 * n + b + 1)
                        v.copy_predicated(half(Xc, b), half_mask(7 + 2 * n, True), bank(2, b)).then_inc(S("x_level"), 1)
                if blk2 and n == 0:
                    dve_group_centre(dve, 0)
                if blk2 and n >= 1:
                    tail(dve, CK, OUT, OUT_PER, 0, n - 1)
                if blk2 and n == 2:
                    dve_group_scale(dve, 0)
                if blk2 and n == 4:
                    dve_group_scaled(dve, 0)
            for b in range(2):
                dve.wait_ge(S("chunk_av"), 2 * blk2 + b + 1)
                for cp, r in ((0, 0), (1, 3)):
                    R = slice(cp * C, cp * C + C)
                    v.tensor_copy(half(Fc, b)[R], bank(r, b)[R]).then_inc(S("chunk_av_out"), 1)
            for cp in range(2):
                n = 2 * blk2 + cp
                R = slice(cp * C, cp * C + C)
                if n:
                    for b in range(2):
                        dve.wait_ge(S("chunk_as"), 2 * n - 1 + b)
                        dve.wait_ge(S("chunk_av_out"), 4 * blk2 + 2 * b + 2)
                        v.tensor_tensor(half(Fc, b)[R], bank(0, b)[R], half(Fc, b)[R], ALU.add
                                        ).then_inc(S("chunk_f_out"), 1)
                for b in range(2):
                    dve.wait_ge(S("chunk_u"), 2 * n + b + 1)
                    v.tensor_copy(half(Uc, b)[R], bank(1, b)[R]).then_inc(S("chunk_u_out"), 1)
                s5 = ps[:, 5, 0:384].rearrange("p (j c) -> p j c", c=C)
                w = spread(wc[:, :, n], C)

                def new_state():
                    dve.wait_ge(S("chunk_s"), n + 1)
                    if n == 0:
                        v.tensor_tensor(ST[:], s5, w, ALU.mult).then_inc(S("chunk_state"), 1)
                    else:
                        dve.wait_ge(S("chunk_rs"), n)
                        link(v.tensor_tensor(ST[:], s5, ST[:], ALU.add), dve)
                        v.tensor_tensor(ST[:], ST[:], w, ALU.mult).then_inc(S("chunk_state"), 1)

                def new_y():
                    y = pvr[:, :, n * C:n * C + C]
                    dve.wait_ge(S("chunk_o"), n + 1)
                    v.tensor_copy(y, ps[:, 4, 0:384].rearrange("p (j c) -> p j c", c=C)).then_inc(S("chunk_y"), 1)
                    if n:
                        dve.wait_ge(S("chunk_rs"), n)
                        dve.wait_ge(S("chunk_y"), 2 * n)
                        v.tensor_tensor(y, ps[:, 6, 0:384].rearrange("p (j c) -> p j c", c=C), y, ALU.add
                                        ).then_inc(S("chunk_y"), 1)
                if n < 3:
                    new_state()
                    new_y()
                else:
                    new_y()
                    new_state()
                dve.wait_ge(S("chunk_state"), n + 1)
        dve.wait_ge(S("sample_turned_y"), 1)
        v.tensor_copy(pvr[:, :, T:N].rearrange("p j b -> p b j"),
                      ps[:, 7, 0:48].rearrange("p (b j) -> p b j", b=NB)).then_inc(S("sample_y_placed"), 1)
        dve.wait_ge(S("chunk_y"), 7)
        dve_group_centre(dve, 1)
        dve_group_scale(dve, 1)
        dve_group_scaled(dve, 1)
        dve.wait_ge(S("group_scaled"), 2)
        dve_rwkv_tail(dve, 0)
        group_gate(dve, v, 1, lambda instrs: linked(instrs, dve))
        dve_rwkv_tail(dve, 1)

    def act_rwkv(act):
        act_gates(act)
        act_chunks(act)

    def dve_rwkv(dve):
        dve_gates(dve)
        dve_chunks(dve)

    def pe_rwkv(pe):
        pe_gates(pe)
        pe_chunks(pe)

    @block.sync
    def _(sp):
        sp_start(sp)
        sp_ffn(sp, *FFN[0])
        sp_in(sp)
        sp_out(sp)
        sp_ffn(sp, *FFN[1])

    @block.scalar
    def _(act):
        act_start(act)
        act_ffn(act, *FFN[0][:3])
        act_in(act)
        act_rwkv(act)
        act_out(act)
        act_ffn(act, *FFN[1][:3])

    @block.vector
    def _(dve):
        dve_start(dve)
        dve_ffn(dve, *FFN[0][:3])
        dve_in(dve)
        project(dve, MT // 2 - 1, 0)
        dve_rwkv(dve)
        dve_out(dve)
        dve_ffn(dve, *FFN[1][:3])

    @block.tensor
    def _(pe):
        pe_start(pe)
        pe_ffn(pe, *FFN[0][:3])
        pe_in(pe)
        pe_shift(pe)
        pe_rwkv(pe)
        pe_out(pe)
        pe_ffn(pe, *FFN[1][:3])

    @block.gpsimd
    def _(pool):
        pool_start(pool)
        pool_squares(pool, 0)
        pool_squares(pool, 1)
        pool_attention(pool)
        pool_state_rows(pool)
        pool_rwkv(pool)
        pool_squares(pool, 2)
        pool_y(pool)

    ctx.close()


_INS = ['x_prompt', 'x_sample', 'cache_swa_k', 'cache_swa_v', 'state_wkv', 'state_shift', 'state_conv',
        'ffn1_norm', 'ffn1_w_gate', 'ffn1_w_up', 'ffn1_w_down', 'mix_norm', 'w_in', 'q_norm', 'k_norm',
        'rwkv_mu', 'rwkv_w0', 'rwkv_w2', 'rwkv_a0', 'rwkv_a2', 'rwkv_g2', 'rwkv_k_k', 'rwkv_k_a', 'rwkv_r_k',
        'rwkv_ln_w', 'rwkv_ln_b', 'conv_w', 'conv_b', 'w_out',
        'ffn2_norm', 'ffn2_w_gate', 'ffn2_w_up', 'ffn2_w_down']
_OUTS = [((1, 256, 2048), 'float32'), ((8, 1, 2048), 'float32'),
         ((1, 1, 256, 8, 64), 'float32'), ((1, 1, 256, 8, 64), 'float32'),
         ((1, 1, 12, 64, 64), 'float32'), ((1, 1, 2560), 'float32'), ((1, 1, 2, 768), 'float32'),
         ((1, 8, 1, 8, 64), 'float32'), ((1, 8, 1, 8, 64), 'float32'),
         ((1, 8, 12, 64, 64), 'float32'), ((1, 8, 2560), 'float32'), ((1, 8, 2, 768), 'float32')]


def kernel(**inputs):
    import numpy as _np
    import concourse.bacc as _bacc
    from concourse import mybir as _mybir
    from concourse.bass_utils import run_bass_kernel_spmd as _run

    nc = _bacc.Bacc("TRN2", target_bir_lowering=False, num_devices=1)
    arrays, args, outs = {}, {}, []
    for name in _INS:
        arrays[f"in_{name}_dram"] = _np.ascontiguousarray(inputs[name])
    for name, a in tables().items():
        arrays[f"in_{name}_dram"] = _np.ascontiguousarray(a)
    for name, a in arrays.items():
        args[name[3:-5]] = nc.dram_tensor(name, a.shape, _mybir.dt.from_np(a.dtype), kind="ExternalInput").ap()
    for i, (shape, dtype) in enumerate(_OUTS):
        dt = _mybir.dt.from_np(_np.dtype(dtype))
        outs.append(nc.dram_tensor(f"out_{i}_dram", shape, dt, kind="ExternalOutput").ap())
    build(nc, args, outs)
    r = _run(nc, [arrays], core_ids=[0])
    return tuple(r.results[0][f"out_{i}_dram"] for i in range(len(_OUTS)))
```
